# Optimizing a Trainium2 kernel written in Bass

```python
import jax, jax.numpy as jnp
from jax import lax
import numpy as np

D_MODEL = 1024
BATCH = 1
SEQ = 512
DEPTH = 1

HEAD_DIM = 64
N_Q_HEADS = D_MODEL // HEAD_DIM
N_KV_HEADS = N_Q_HEADS // 4
D_CONV = D_MODEL
CONV_WIDTH = 3
WINDOW = 128
BLOCK = 128
D_FF = ((8 * D_MODEL // 3 + 127) // 128) * 128
EPS = 1e-6
SPLITS = [D_CONV, D_CONV, D_CONV,
          N_Q_HEADS * HEAD_DIM, N_KV_HEADS * HEAD_DIM, N_KV_HEADS * HEAD_DIM,
          D_MODEL, D_MODEL]
D_IN = sum(SPLITS)

kernel_name = "hybrid_gated_conv_swa_encoder_block"

def rms_norm(x, gain):
    xf = x.astype(jnp.float32)
    y = xf * lax.rsqrt(jnp.mean(xf * xf, axis=-1, keepdims=True) + EPS)
    return (y * gain.astype(jnp.float32)).astype(x.dtype)

def dwconv3(x, w):
    ch = x.shape[-1]
    pad = (CONV_WIDTH - 1) // 2
    return lax.conv_general_dilated(
        x, w.astype(x.dtype)[:, None, :], window_strides=(1,),
        padding=((pad, pad),), dimension_numbers=("NWC", "WIO", "NWC"),
        feature_group_count=ch)

def alibi_slopes(n_heads):
    return jnp.asarray(2.0 ** (-8.0 * np.arange(1, n_heads + 1) / n_heads), dtype=jnp.float32)

def windowed_gqa(q, k, v, sink):
    b, s, _, hd = q.shape
    g = N_Q_HEADS // N_KV_HEADS
    nb = s // BLOCK
    qb = q.reshape(b, nb, BLOCK, N_KV_HEADS, g, hd)

    def band(t):
        tp = jnp.pad(t, ((0, 0), (BLOCK, BLOCK), (0, 0), (0, 0)))
        tp = tp.reshape(b, nb + 2, BLOCK, N_KV_HEADS, hd)
        return jnp.concatenate([tp[:, :-2], tp[:, 1:-1], tp[:, 2:]], axis=2)

    kb, vb = band(k), band(v)
    scores = jnp.einsum('bnqkgd,bnjkd->bkgnqj', qb, kb).astype(jnp.float32)
    scores = scores * (1.0 / np.sqrt(hd)).astype(np.float32)

    blk = jnp.arange(nb)[:, None]
    qpos = blk * BLOCK + jnp.arange(BLOCK)[None, :]
    kpos = (blk - 1) * BLOCK + jnp.arange(3 * BLOCK)[None, :]
    dist = jnp.abs(qpos[:, :, None] - kpos[:, None, :])
    valid = (dist <= WINDOW) & (kpos[:, None, :] >= 0) & (kpos[:, None, :] < s)
    slopes = alibi_slopes(N_Q_HEADS).reshape(N_KV_HEADS, g, 1, 1, 1)
    bias = -slopes * dist.astype(jnp.float32)[None, None]
    scores = jnp.where(valid[None, None], scores + bias[None], -1e30)

    sink_b = sink.astype(jnp.float32).reshape(1, N_KV_HEADS, g, 1, 1, 1)
    m = jnp.maximum(jnp.max(scores, axis=-1, keepdims=True), sink_b)
    p = jnp.exp(scores - m)
    p = p / (jnp.sum(p, axis=-1, keepdims=True) + jnp.exp(sink_b - m))
    out = jnp.einsum('bkgnqj,bnjkd->bnqkgd', p.astype(v.dtype), vb)
    return out.reshape(b, s, N_Q_HEADS * hd)

def token_mixer(h, w_in, conv_w, q_gain, k_gain, sink, w_o):
    b, s, _ = h.shape
    proj = h @ w_in
    cb, cc, cu, q, k, v, ga, gb = jnp.split(proj, np.cumsum(SPLITS)[:-1].tolist(), axis=-1)
    y_a = cb * dwconv3(cc * cu, conv_w)
    q = rms_norm(q.reshape(b, s, N_Q_HEADS, HEAD_DIM), q_gain)
    k = rms_norm(k.reshape(b, s, N_KV_HEADS, HEAD_DIM), k_gain)
    v = v.reshape(b, s, N_KV_HEADS, HEAD_DIM)
    y_b = windowed_gqa(q, k, v, sink)
    merged = jax.nn.sigmoid(ga) * y_a + jax.nn.sigmoid(gb) * y_b
    return merged @ w_o

def conv_ffn(h, w_up, ffn_conv_w, ffn_conv_b, w_down):
    a, gbr = jnp.split(h @ w_up, 2, axis=-1)
    a = dwconv3(a, ffn_conv_w) + ffn_conv_b
    return (jax.nn.gelu(a) * gbr) @ w_down

def setup_inputs(seed: int = 0) -> dict:
    key = jax.random.key(seed)
    ks = jax.random.split(key, 16)
    nrm = jax.random.normal
    f32 = jnp.float32
    L, D = DEPTH, D_MODEL
    return {
        "x": nrm(ks[0], (BATCH, SEQ, D), f32),
        "c": nrm(ks[1], (BATCH, D), f32),
        "w_ada": nrm(ks[2], (L, D, 6 * D), f32) * (0.5 * D ** -0.5),
        "b_ada": nrm(ks[3], (L, 6 * D), f32) * 0.01,
        "norm1_gain": 1.0 + 0.02 * nrm(ks[4], (L, D), f32),
        "w_in": nrm(ks[5], (L, D, D_IN), f32) * D ** -0.5,
        "conv_w": nrm(ks[6], (L, CONV_WIDTH, D_CONV), f32) * CONV_WIDTH ** -0.5,
        "q_gain": 1.0 + 0.02 * nrm(ks[7], (L, HEAD_DIM), f32),
        "k_gain": 1.0 + 0.02 * nrm(ks[8], (L, HEAD_DIM), f32),
        "sink": 0.5 * nrm(ks[9], (L, N_Q_HEADS), f32),
        "w_o": nrm(ks[10], (L, D, D), f32) * D ** -0.5,
        "norm2_gain": 1.0 + 0.02 * nrm(ks[11], (L, D), f32),
        "w_up": nrm(ks[12], (L, D, 2 * D_FF), f32) * D ** -0.5,
        "ffn_conv_w": nrm(ks[13], (L, CONV_WIDTH, D_FF), f32) * CONV_WIDTH ** -0.5,
        "ffn_conv_b": 0.01 * nrm(ks[14], (L, D_FF), f32),
        "w_down": nrm(ks[15], (L, D_FF, D), f32) * D_FF ** -0.5,
    }

def reference(x, c, w_ada, b_ada, norm1_gain, w_in, conv_w, q_gain, k_gain, sink,
              w_o, norm2_gain, w_up, ffn_conv_w, ffn_conv_b, w_down):
    c_act = jax.nn.silu(c)
    for l in range(DEPTH):
        mod = c_act @ w_ada[l] + b_ada[l]
        sh1, sc1, g1, sh2, sc2, g2 = [t[:, None, :] for t in jnp.split(mod, 6, axis=-1)]
        h = rms_norm(x, norm1_gain[l]) * (1.0 + sc1) + sh1
        x = x + g1 * token_mixer(h, w_in[l], conv_w[l], q_gain[l], k_gain[l], sink[l], w_o[l])
        h = rms_norm(x, norm2_gain[l]) * (1.0 + sc2) + sh2
        x = x + g2 * conv_ffn(h, w_up[l], ffn_conv_w[l], ffn_conv_b[l], w_down[l])
    return x


_drawn_inputs = setup_inputs


def setup_inputs(seed=0):
    import zlib

    import numpy as np

    out = dict(_drawn_inputs(seed))
    spreads = {}
    factors = {'b_ada': 4.606,
     'norm1_gain': 7.692,
     'q_gain': 200.0,
     'k_gain': 200.0,
     'sink': 8.0,
     'norm2_gain': 64.0,
     'ffn_conv_b': 200.0}
    for name, (base, spread) in spreads.items():
        noise = np.random.default_rng([zlib.crc32(name.encode()), seed]).standard_normal(out[name].shape)
        drawn = base * np.exp(spread * noise) if base else spread * noise
        out[name] = __import__('jax').numpy.asarray(drawn.astype(out[name].dtype))
    for name, factor in factors.items():
        out[name] = (out[name] * factor).astype(out[name].dtype)
    return out
```

```python
import concourse.bass as bass
from concourse import mybir
from contextlib import ExitStack
import numpy as np


class Tally:

    def __init__(self, eng, sem):
        self.eng, self.sem, self.n, self.turn = eng, sem, 0, 0

    def enter(self, i, per):
        self.start, self.per, self.turn = self.n, per, i * per

    def leave(self, turns):
        assert self.n - self.start == self.per, (self.n - self.start, self.per)
        self.n, self.turn = self.start + turns * self.per, 0

    def inc(self, ins):
        ins.then_inc(self.sem, 1)
        self.n += 1

    def link(self, ins):
        self.inc(ins)
        self.eng.wait_ge(self.sem, self.turn + self.n)


def encoder_block(nc, x, c, w_ada, b_ada, norm1_gain, w_in, conv_w, q_gain, k_gain, sink, w_o,
                  norm2_gain, w_up, ffn_conv_w, ffn_conv_b, w_down, out):
    fp32, f32r = mybir.dt.float32, mybir.dt.float32r
    ALU, ACT, AX = mybir.AluOpType, mybir.ActivationFunctionType, mybir.AxisListType
    MUL, ADD, SUB, MAX = ALU.mult, ALU.add, ALU.subtract, ALU.max

    P = 128
    S, D = x.shape[1], x.shape[2]
    KT = D // P
    NB = S // P
    HD = q_gain.shape[1]
    H = D // HD
    KV = H // 4
    HG = H // KV
    FF = w_down.shape[1]
    FT = FF // P
    PC = 2 * P
    EPS = 1e-6
    BAND = 3 * P
    MASKED = -1e35
    GELU_C, GELU_S = 0.044715, float(np.sqrt(2 / np.pi))
    RS = 1.0 / np.sqrt(HD)

    COL_B, COL_C, COL_U, COL_Q = 0, D, 2 * D, 3 * D
    COL_K = 4 * D
    COL_V = COL_K + KV * HD
    COL_GA = COL_V + KV * HD
    COL_GB = COL_GA + D
    MIX = [COL_Q, COL_C, COL_U, COL_B, COL_GA, COL_GB]
    NM = len(MIX)

    P_MIX = 2
    P_WO = P_MIX + NM * KV
    P_UP = P_WO + D // PC
    P_DOWN = P_UP + 2 * (FF // PC)
    CH = [8, 8, FT - 16]
    P_END = P_DOWN + len(CH) * (D // PC)

    PA_C, PA_B, PA_G1, PA_G2, PA_CW = 0, KT, 7 * KT, 8 * KT, 9 * KT
    PA_QG, PA_KG = 12 * KT, 12 * KT + 1
    ROWS1 = 12 * KT + 2
    PA_FW, PA_FB = ROWS1, ROWS1 + 3 * FT
    ROWS2 = 4 * FT

    def k_rows(w):
        return w[0].rearrange("(k p) n -> p k n", p=P)

    wi, wo, wu, wd = k_rows(w_in), k_rows(w_o), k_rows(w_up), k_rows(w_down)
    out_v = out[0].rearrange("(b p) n -> p b n", p=P)

    ctx = ExitStack()
    with ctx:
        def sb(name, shape, dt=fp32, into=ctx):
            return into.enter_context(nc.sbuf_tensor(name, shape, dt))

        def sem(name):
            return ctx.enter_context(nc.semaphore(name))

        h_hi = sb("h_hi", [P, KT, S], f32r)
        h_lo = sb("h_lo", [P, KT, S], f32r)
        xT = sb("xT", [P, KT, S])
        w_raw = sb("w_raw", [P, 2, 8, PC])
        w_hi = sb("w_hi", [P, 2, 2, 8, P], f32r)
        w_lo = sb("w_lo", [P, 2, 2, 8, P], f32r)
        par = sb("par", [P, ROWS1 + ROWS2])
        mod = sb("mod", [P, 6 * KT])
        amp = sb("amp", [P, 2, KT])
        c_act = sb("c_act", [P, 2, KT])
        ident = sb("ident", [P, P])
        ones = sb("ones", [P, P])
        half = sb("half", [P, 2])
        sink_b = sb("sink_b", [P, H])
        ndist = sb("ndist", [P, BAND])
        st = sb("st", [P, 8, 16])
        sm = sb("sm", [P, 7, NB, HG])
        a_buf = sb("a_buf", [P, 2, S])
        b_buf = sb("b_buf", [P, 2, S])
        y_buf = sb("y_buf", [P, 2, S])
        pad_f = sb("pad_f", [P, 2 * (S + 2)])
        pad = [pad_f[:, u * (S + 2):(u + 1) * (S + 2)] for u in range(2)]

        start = ExitStack()
        x_nat = sb("x_nat", [P, NB, D], into=start)
        xn = sb("xn", [P, NB, D], into=start)
        hT = sb("hT", [P, KT, S], into=start)
        ada0 = sb("ada0", [P, 4, 2 * D], into=start)
        acc0 = sb("acc0", [P, 2 * D], into=start)
        start.close()

        mixer = ExitStack()
        merged = sb("merged", [P, KT, S], into=mixer)
        k_st = sb("k_st", [P, 2, KV, S], f32r, into=mixer)
        v_nat = sb("v_nat", [P, NB, KV * HD], into=mixer)
        q_st = sb("q_st", [P, HG, S], f32r, into=mixer)
        v_hi = sb("v_hi", [P, NB, 2, HD], f32r, into=mixer)
        v_lo = sb("v_lo", [P, NB, 2, HD], f32r, into=mixer)
        bias = sb("bias", [P, HG, BAND], into=mixer)
        prob = sb("prob", [P, 2, HG, BAND], into=mixer)
        pt_hi = sb("pt_hi", [P, 2, HG * P], f32r, into=mixer)
        pt_lo = sb("pt_lo", [P, 2, HG * P], f32r, into=mixer)
        ada = sb("ada", [P, 2, D], into=mixer)
        acc = sb("acc", [P, D], into=mixer)
        mixer.close()
        k_nat = prob[:, 0, :, :].rearrange("p h j -> p (h j)")[:, 0:NB * KV * HD]
        k_sq = prob[:, 1, :, :].rearrange("p h j -> p (h j)")[:, 0:NB * KV * HD]
        k_T = merged[:, 0:2, :]

        channel = ExitStack()
        g_hi = sb("g_hi", [P, FT, S], f32r, into=channel)
        g_lo = sb("g_lo", [P, FT, S], f32r, into=channel)
        channel.close()
        par_rows = w_raw[:, 1, :, :].rearrange("p k n -> p (k n)")

        bank = [ctx.enter_context(nc.psum_tensor(f"bank{i}", [P, S], fp32)) for i in range(8)]
        SC, TB, OB, MB = (2, 3), (4, 5), 6, 7

        par_in, sink_in = sem("par_in"), sem("sink_in")
        x_in = [sem(f"x_in{b}") for b in range(NB)]
        ada0_in = [sem(f"ada0_in{k}") for k in range(4)]
        ada_in = [sem(f"ada_in{k}") for k in range(2)]
        w_in_slot = [sem(f"w_loaded{s}") for s in range(2)]
        out_dma = [sem(f"out_stored{s}") for s in range(2)]
        const_done = sem("const_done")
        half_done = sem("half_done")
        dist_done = sem("dist_done")
        bias_done = sem("bias_done")
        hi_ready = sem("hi_ready")
        lo_ready = sem("lo_ready")
        units_done = sem("units_done")
        par_t, par_c = sem("par_transposed"), sem("par_copied")
        x_sq, x_n = sem("x_squared"), sem("x_normed")
        xt_done, xt_out = sem("x_transposed"), sem("xt_copied")
        gemv_done, mod_done = sem("gemv_done"), sem("mod_summed")
        h_f, h_h, h_ready = sem("h_float"), sem("h_high"), sem("h_ready")
        var_ready, root_ready = sem("var_ready"), sem("root_ready")
        kn_ready, kt_done, kh_done, kl_done = sem("k_normed"), sem("k_transposed"), sem("k_high"), sem("k_low")
        g_act, g_dve = sem("drained_by_act"), sem("drained_by_dve")
        score_free, t_free, o_free, m_free = sem("score_free"), sem("t_free"), sem("o_free"), sem("m_free")
        mix_free = sem("mix_free")
        q_sq, q_hi, q_lo = sem("q_squared"), sem("q_high"), sem("q_low")
        ssq_done, s_done, t_done, pt_h, pv_done = (sem("q_sums"), sem("scores"), sem("p_transposed"),
                                                   sem("pt_high"), sem("pv"))
        v_staged, shift_ready, exp_done, p_ready = sem("v_staged"), sem("shift_ready"), sem("exp_done"), sem("p_ready")
        ma_done = sem("branch_a_gated")
        m_hi, m_lo = sem("merged_high"), sem("merged_low")
        x2_done, x2_sq, sum_done, ss_done, diag_done, r_done = (sem("x2"), sem("x2_squared"), sem("x2_summed"),
                                                                sem("norm2_sums"), sem("diag"), sem("rstd_spread"))
        t2_done, h2_h, h2_ready = sem("h2_scaled"), sem("h2_high"), sem("h2_ready")
        a_free, b_free = sem("act_drained_ffn"), sem("dve_drained_ffn")
        conv_done, f_sq, z_done, f_th = sem("ffn_conv"), sem("ffn_squared"), sem("gelu_arg"), sem("gelu_tanh")
        ffn_tiles = sem("ffn_tiles")
        yt_done = sem("y_transposed")
        act_done, dve_done, pool_done = sem("act_steps"), sem("dve_steps"), sem("pool_steps")

        def at(i, per, n):
            return n if i is None else i * per + n

        TS = [[0, 1], [2, 3, 4], [5, 6, 7], [8, 9]]
        NT = 10
        STEPS, STEPS_UP = 35, 8

        block = ctx.enter_context(nc.Block())

        @block.sync
        def _(sp):
            def load(i, per, n, src):
                if n >= 2:
                    sp.wait_ge(lo_ready, at(i, 2 * per, 2 * n - 2))
                sp.dma_start(w_raw[:, n % 2, 0:src.shape[1], :], src).then_inc(w_in_slot[n % 2], 16)

            for b in range(NB):
                sp.dma_start(x_nat[:, b, :], x[0, b * P:(b + 1) * P, :]).then_inc(x_in[b], 16)
            for k in range(KT):
                if k >= 4:
                    sp.wait_ge(gemv_done, k - 3)
                sp.dma_start(ada0[:, k % 4, :], w_ada[0, k * P:(k + 1) * P, 0:2 * D]).then_inc(ada0_in[k % 4], 16)
                if k == 5:
                    load(None, 0, 0, wi[:, :, COL_K:COL_K + PC])
            sp.wait_ge(par_t, 2)
            load(None, 0, 1, wi[:, :, COL_V:COL_V + PC])
            sp.wait_ge(h_ready, KT)
            with sp.Fori(1, KV + 1) as g1:
                g = g1 - 1
                for n in range(NM):
                    load(g, NM, P_MIX + n, wi[:, :, bass.ds(g1 * PC + (MIX[n] - PC), PC)])
                    for k in ([0, 1], [2], [3], [4, 5], [6], [7])[n]:
                        sp.wait_ge(gemv_done, g * KT + (KT + k - 1))
                        sp.dma_start(ada[:, k % 2, :],
                                     w_ada[0, k * P:(k + 1) * P, bass.ds(g1 * D + D, D)]).then_inc(ada_in[k % 2], 16)
            for n in range(D // PC):
                load(None, 0, P_WO + n, wo[:, :, n * PC:(n + 1) * PC])
            with sp.Fori(1, FF // PC + 1) as j1:
                j = j1 - 1
                for n in range(2):
                    load(j, 2, P_UP + n, wu[:, :, bass.ds(j1 * PC + (n * FF - PC), PC)])
            with sp.Fori(1, 3) as i1:
                i = i1 - 1
                for n in range(6):
                    q, k0 = n // 3, 8 * (n % 3)
                    load(i, 6, P_DOWN + n, wd[:, k0:k0 + CH[n % 3], bass.ds(i1 * (2 * PC) + (q - 2) * PC, PC)])

        @block.gpsimd
        def _(pool):
            steps = Tally(pool, pool_done)

            def low(i, per, n):
                for u in range(2):
                    pool.wait_ge(hi_ready, at(i, 2 * per, 2 * n + u + 1))
                    pool.tensor_tensor(w_lo[:, n % 2, u], w_raw[:, n % 2, :, u * P:(u + 1) * P],
                                       w_hi[:, n % 2, u], SUB).then_inc(lo_ready, 1)

            steps.link(pool.memset(ident[:, :], 0.0))
            pool.affine_select(out=ident[:, :], in_=ident[:, :], compare_op=ALU.not_equal, fill=1.0, base=0,
                               pattern=[[-1, P]], channel_multiplier=1).then_inc(const_done, 1)
            pool.memset(ones[:, :], 1.0).then_inc(const_done, 1)
            pool.iota(ndist[:, :], pattern=[[-1, BAND]], base=P, channel_multiplier=1,
                      allow_small_or_imprecise_dtypes=True).then_inc(const_done, 1)
            pool.wait_ge(dist_done, 1)
            steps.link(pool.affine_select(out=ndist[:, :], in_=ndist[:, :], compare_op=ALU.is_ge, fill=MASKED,
                                          base=2 * P, pattern=[[-1, BAND]], channel_multiplier=1))
            steps.link(pool.affine_select(out=ndist[:, :], in_=ndist[:, :], compare_op=ALU.is_ge, fill=MASKED,
                                          base=0, pattern=[[1, BAND]], channel_multiplier=-1))
            low(None, 0, 0)
            low(None, 0, 1)
            pool.wait_ge(h_ready, KT)
            for h in range(HG):
                slope = float(np.float32(2.0 ** (-8.0 * (h + 1) / H)))
                pool.tensor_scalar(bias[:, h, :], ndist[:, :], slope, None, MUL).then_inc(bias_done, 1)
            low(None, 0, 2)
            with pool.Fori(0, KV) as g:
                for n in range(NM):
                    if n == 5:
                        pool.wait_ge(score_free, g * (NB * HG) + (NB * HG + 2))
                    low(g, NM, P_MIX + n + 1)
                    if n == 5:
                        pool.tensor_scalar(bias[:, :, :], bias[:, :, :], 2.0 ** (-8 * HG // H), None,
                                           MUL).then_inc(bias_done, 1)
            for n in range(P_WO + 1, P_UP + 1):
                low(None, 0, n)
            with pool.Fori(0, FF // PC) as j:
                for n in range(2):
                    low(j, 2, P_UP + n + 1)
            for n in range(P_DOWN + 1, P_END):
                low(None, 0, n)

        @block.scalar
        def _(act):
            steps = Tally(act, act_done)

            def high(i, per, n, units=(0, 1)):
                act.wait_ge(w_in_slot[n % 2], at(i, 16 * per // 2, 16 * (n // 2) + 16))
                if n >= 2:
                    act.wait_ge(units_done, at(i, 2 * per, 2 * n - 2))
                for u in units:
                    act.activation(w_hi[:, n % 2, u], w_raw[:, n % 2, :, u * P:(u + 1) * P],
                                   ACT.Copy).then_inc(hi_ready, 1)

            rows = 0
            for src, n in ((c[0:1, :], KT), (b_ada, 6 * KT), (norm1_gain, KT), (norm2_gain, KT), (conv_w[0], 3 * KT)):
                act.dma_start(par_rows[rows:rows + n, 0:P],
                              src.rearrange("a (f p) -> (a f) p", p=P)).then_inc(par_in, 16)
                rows += n
            for r, src in enumerate((q_gain, k_gain)):
                for a in range(2):
                    act.dma_start(par_rows[rows + r:rows + r + 1, a * HD:(a + 1) * HD], src).then_inc(par_in, 16)
            act.dma_start(par_rows[0:3 * FT, P:2 * P],
                          ffn_conv_w[0].rearrange("a (f p) -> (a f) p", p=P)).then_inc(par_in, 16)
            act.dma_start(par_rows[3 * FT:4 * FT, P:2 * P],
                          ffn_conv_b.rearrange("a (f p) -> (a f) p", p=P)).then_inc(par_in, 16)
            act.dma_start(sink_b[:, :], sink.to_broadcast([P, H])).then_inc(sink_in, 16)

            for t, (r0, n) in enumerate(((0, ROWS1), (ROWS1, ROWS2))):
                act.wait_ge(par_t, t + 1)
                act.activation(par[:, r0:r0 + n], bank[6 + t][:, 0:n], ACT.Copy).then_inc(par_c, 1)
            act.wait_ge(par_c, 1)
            act.activation(c_act[:, 1, :], par[:, PA_C:PA_C + KT], ACT.Tanh, scale=0.5).then_inc(par_c, 1)
            for b in range(NB):
                act.wait_ge(x_in[b], 16)
                act.activation(xn[:, b, :], x_nat[:, b, :], ACT.Square, accum_out=st[:, 0, b:b + 1]).then_inc(x_sq, 1)
            roots = 0

            def root(i, per, n, cols, src, dst):
                act.wait_ge(var_ready, at(i, per, n + 1))
                act.activation(st[:, dst, 0:cols], st[:, src, 0:cols], ACT.Sqrt).then_inc(root_ready, 1)

            root(None, 0, 0, NB, 1, 2)
            for m in range(2 * KT):
                act.wait_ge(xt_done, m + 1)
                act.activation((xT if m < KT else hT)[:, m % KT, :], bank[m % 4][:, :], ACT.Copy).then_inc(xt_out, 1)
            high(None, 0, 0)
            for k in range(KT):
                act.wait_ge(h_f, k + 1)
                act.activation(h_hi[:, k, :], hT[:, k, :], ACT.Copy).then_inc(h_h, 1)
            high(None, 0, 1)
            act.wait_ge(units_done, 2)
            act.wait_ge(h_ready, KT)
            for b in range(NB):
                act.activation(k_nat[:, b * PC:(b + 1) * PC], bank[b][:, 0:PC], ACT.Copy).then_inc(g_act, 1)
            high(None, 0, 2)
            root(None, 0, 1, NB * KV, 1, 2)
            act.wait_ge(units_done, 4)
            act.activation(v_nat[:, 2, :], bank[6][:, 0:PC], ACT.Copy).then_inc(o_free, 1)
            for j in range(KV):
                act.wait_ge(score_free, j // 2 + 1)
                a = (j % 2) * HD
                for o in range(2):
                    act.activation(k_st[o * HD:(o + 1) * HD, 0, j, :], k_T[a:a + HD, j // 2, :],
                                   ACT.Copy).then_inc(kh_done, 1)

            with act.Fori(0, KV) as g:
                U = 2 * P_MIX

                def unit(n):
                    act.wait_ge(units_done, g * (2 * NM) + (U + n + 1))

                def query(u):
                    unit(u)
                    act.wait_ge(mix_free, g * 2 + 2)
                    act.activation(y_buf[:, u, :], bank[u][:, :], ACT.Copy).then_inc(g_act, 1)
                    act.wait_ge(g_act, g * 8 + (NB + u + 1))
                    act.activation(b_buf[:, u, :], y_buf[:, u, :], ACT.Square).then_inc(q_sq, 1)
                    for o in range(2):
                        r = slice(o * HD, (o + 1) * HD)
                        act.activation(q_st[r, 2 * u + o, :], y_buf[r, u, :], ACT.Copy).then_inc(q_hi, 1)

                def conv_c(u):
                    unit(2 + u)
                    act.activation(a_buf[:, u, :], bank[u][:, :], ACT.Copy).then_inc(g_act, 1)

                def exps(b):
                    w = BAND if 0 < b < NB - 1 else 2 * P
                    act.wait_ge(shift_ready, g * NB + (b + 1))
                    for h in range(HG):
                        act.activation(prob[:, b % 2, h, 0:w], prob[:, b % 2, h, 0:w], ACT.Exp,
                                       bias=sm[:, 1, b, h:h + 1], accum_out=sm[:, 3, b, h:h + 1]).then_inc(exp_done, 1)
                    act.activation(sm[:, 4, b, :], sm[:, 2, b, :], ACT.Exp).then_inc(exp_done, 1)

                def turned_high(ts):
                    for t in ts:
                        act.wait_ge(t_done, g * NT + (t + 1))
                        act.activation(pt_hi[:, t % 2, :], bank[TB[t % 2]][:, :], ACT.Copy).then_inc(pt_h, 1)

                def heads_out(b):
                    act.wait_ge(pv_done, g * NB + (b + 1))
                    for o in range(2):
                        r = slice(o * HD, (o + 1) * HD)
                        act.activation(y_buf[r, :, b * P:(b + 1) * P],
                                       bank[OB][r, :].rearrange("p (u o q) -> p u o q", u=2, o=2)[:, :, o, :],
                                       ACT.Copy).then_inc(o_free, 1)

                def gate(n):
                    unit(n)
                    if n >= 10:
                        act.wait_ge(ma_done, g * 2 + (n - 9))
                    act.activation(b_buf[:, n % 2, :], bank[n % 2][:, :], ACT.Tanh, scale=0.5).then_inc(g_act, 1)

                high(g, NM, P_MIX + 1)
                query(0)
                query(1)
                high(g, NM, P_MIX + 2)
                conv_c(0)
                root(g, 1, 2, NB * HG, 1, 2)
                conv_c(1)
                high(g, NM, P_MIX + 3)
                exps(0)
                turned_high(TS[0])
                high(g, NM, P_MIX + 4)
                exps(1)
                heads_out(0)
                turned_high(TS[1][:2])
                exps(2)
                turned_high(TS[1][2:])
                high(g, NM, P_MIX + 5)
                heads_out(1)
                gate(8)
                turned_high(TS[2][:2])
                exps(3)
                turned_high(TS[2][2:])
                high(g, NM, P_MIX + 6)
                gate(9)
                heads_out(2)
                turned_high(TS[3])
                gate(10)
                heads_out(3)
                gate(11)

            act.wait_ge(units_done, 2 * P_WO)
            for k in range(KT):
                act.wait_ge(mix_free, k + 3)
                act.activation(h_hi[:, k, :], merged[:, k, :], ACT.Copy, scale=0.5).then_inc(m_hi, 1)
            for n in range(D // PC):
                high(None, 0, P_WO + n + 1)
                for f in (2 * n, 2 * n + 1):
                    if f in (4, 5):
                        act.wait_ge(b_free, f - 3)
                    else:
                        act.wait_ge(x2_done, f + 1 if f < 4 else f - 1)
                    if f >= 2:
                        act.wait_ge(sum_done, max(f - 2, 1))
                    act.activation(b_buf[:, f % 2, :], xT[:, f, :],
                                   ACT.Square).then_inc(a_free if f in (2, 3) else x2_sq, 1)
            root(None, 0, 2 + KV, NB, 1, 2)
            for f in range(KT):
                act.wait_ge(t2_done, f + 1)
                act.activation(h_hi[:, f, :], a_buf[:, f % 2, :], ACT.Identity,
                               bias=mod[:, 3 * KT + f:3 * KT + f + 1]).then_inc(h2_h, 1)

            with act.Fori(0, FF // PC) as j:
                U = 2 * P_UP
                high(j, 2, P_UP + 1)
                for u in range(2):
                    act.wait_ge(units_done, j * 4 + (U + u + 1))
                    act.activation(pad[u][:, 1:S + 1], bank[2 + u][:, :], ACT.Copy).then_inc(a_free, 1)
                high(j, 2, P_UP + 2)
                for u in range(2):
                    act.wait_ge(conv_done, j * 2 + (u + 1))
                    act.activation(b_buf[:, u, :], a_buf[:, u, :], ACT.Square).then_inc(f_sq, 1)
                for u in range(2):
                    act.wait_ge(z_done, j * 2 + (u + 1))
                    act.activation(b_buf[:, u, :], b_buf[:, u, :], ACT.Tanh,
                                   scale=GELU_C * GELU_S).then_inc(f_th, 1)

            def store(q):
                stage = stages[q % 2]
                if q >= 2:
                    act.wait_ge(out_dma[q % 2], 16)
                for u in range(2):
                    act.wait_ge(yt_done, 2 * q + u + 1)
                    act.activation(stage[:, :, u * P:(u + 1) * P],
                                   bank[4 + 2 * (q % 2) + u][:, :].rearrange("p (b n) -> p b n", b=NB),
                                   ACT.Copy).then_inc(a_free, 1)
                act.wait_ge(a_free, 2 + 2 * FF // PC + 2 * q + 2)
                act.dma_start(out_v[:, :, q * PC:(q + 1) * PC], stage).then_inc(out_dma[q % 2], 16)

            stages = [b_buf[:, :, :].rearrange("p u s -> p (u s)").rearrange("p (b n) -> p b n", b=NB),
                      pad_f[:, 0:2 * S].rearrange("p (b n) -> p b n", b=NB)]
            for n in range(P_DOWN, P_END):
                if n + 1 < P_END:
                    high(None, 0, n + 1)
                if n == P_DOWN + 4:
                    store(0)
                if n == P_DOWN + 6:
                    store(1)
                if n == P_DOWN + 10:
                    store(2)
            store(3)
            for s in range(2):
                act.wait_ge(out_dma[s], 32)

        @block.tensor
        def _(pe):
            def three(dst, w_h, w_l, rhs_hi, rhs_lo, first, last):
                pe.matmul(dst, w_h, rhs_hi, start=first, stop=False)
                pe.matmul(dst, w_h, rhs_lo, start=False, stop=False)
                return pe.matmul(dst, w_l, rhs_hi, start=False, stop=last)

            pe.wait_ge(const_done, 1)
            pe.wait_ge(par_in, 16 * 11)
            for t, n in enumerate((ROWS1, ROWS2)):
                pe.transpose(bank[6 + t][:, 0:n], par_rows[0:n, t * P:(t + 1) * P], ident[0:n, 0:n]).then_inc(par_t, 1)
            for b in range(NB):
                pe.wait_ge(x_in[b], 16)
            for m in range(2 * KT):
                if m == KT:
                    pe.wait_ge(x_n, NB)
                if m >= 4:
                    pe.wait_ge(xt_out, m - 3)
                for b in range(NB):
                    mm = pe.transpose(bank[m % 4][:, b * P:(b + 1) * P],
                                      (x_nat if m < KT else xn)[:, b, (m % KT) * P:(m % KT + 1) * P], ident[:, :])
                mm.then_inc(xt_done, 1)
            pe.wait_ge(const_done, 2)
            pe.wait_ge(par_c, 1)
            pe.wait_ge(gemv_done, KT)
            for f in range(2 * KT):
                mm = pe.matmul(bank[6][:, f:f + 1], acc0[:, f * P:(f + 1) * P], ones[:, 0:1], start=True, stop=True)
            mm.then_inc(mod_done, 1)

            for n in range(2):
                pe.wait_ge(lo_ready, 2 * n + 2)
                if n == 1:
                    pe.wait_ge(par_c, 2)
                for k in range(KT):
                    if n == 0:
                        pe.wait_ge(h_ready, k + 1)
                    for b in range(NB):
                        dst = bank[4 * n + b][:, 0:PC].rearrange("p (u n) -> p u n", u=2)
                        t = slice(b * P, (b + 1) * P)
                        mm = three(dst, h_hi[:, k, t], h_lo[:, k, t], w_hi[:, n, :, k, :], w_lo[:, n, :, k, :],
                                   k == 0, k == KT - 1)
                        if k == KT - 1 and b >= 2:
                            mm.then_inc(units_done, 1)
            pe.wait_ge(kn_ready, 1)
            for f in range(2):
                for b in range(NB):
                    mm = pe.transpose(bank[SC[f]][:, b * P:(b + 1) * P],
                                      k_nat[:, b * PC + f * P:b * PC + (f + 1) * P], ident[:, :])
                mm.then_inc(kt_done, 1)

            pe.wait_ge(half_done, 2)
            with pe.Fori(0, KV) as g:
                def unit_waits(n):
                    pe.wait_ge(lo_ready, g * (2 * NM) + (2 * P_MIX + n + 1))
                    if n in (6, 7, 8, 9):
                        pe.wait_ge(g_dve, g * 4 + (n - 5))
                    else:
                        pe.wait_ge(g_act, g * 8 + {0: 3, 1: 4, 2: 5, 3: 6, 4: 7, 5: 8, 10: 9, 11: 10}[n])

                def unit_half(n, a):
                    s, u = (n // 2) % 2, n % 2
                    for k in range(4 * a, 4 * a + 4):
                        mm = three(bank[u][:, :], w_hi[:, s, u, k, :], w_lo[:, s, u, k, :],
                                   h_hi[:, k, :], h_lo[:, k, :], k == 0, k == KT - 1)
                    if a:
                        mm.then_inc(units_done, 1)

                def square_sums():
                    pe.wait_ge(q_sq, g * 2 + 2)
                    pe.wait_ge(m_free, g * 2 + 1)
                    for u in range(2):
                        for b in range(NB):
                            mm = pe.matmul(bank[MB][:, b * HG + 2 * u:b * HG + 2 * u + 2],
                                           b_buf[:, u, b * P:(b + 1) * P], half[:, :], start=True, stop=True)
                    mm.then_inc(ssq_done, 1)

                def scores(b, hs):
                    j0, j1 = max(b - 1, 0) * P, min(b + 2, NB) * P
                    for h in hs:
                        pe.wait_ge(q_lo, g * HG + (h + 1))
                        pe.wait_ge(score_free, g * (NB * HG) + (b * HG + h + 1))
                        dst = bank[SC[h % 2]][:, 0:j1 - j0]
                        for p in range(2):
                            mm = pe.matmul(dst, q_st[:, h, b * P:(b + 1) * P],
                                           k_st[:, p, bass.ds(g, 1), j0:j1].rearrange("p a n -> p (a n)"),
                                           start=(p == 0), stop=(p == 1))
                        mm.then_inc(s_done, 1)

                def turn(b, i):
                    t = TS[b][i]
                    pe.wait_ge(p_ready, g * (NB * HG) + (b * HG + HG))
                    pe.wait_ge(t_free, g * NT + (t + 1))
                    for h in range(HG):
                        mm = pe.transpose(bank[TB[t % 2]][:, h * P:(h + 1) * P],
                                          prob[:, b % 2, h, i * P:(i + 1) * P], ident[:, :])
                    mm.then_inc(t_done, 1)

                def values(b, i):
                    t = TS[b][i]
                    pe.wait_ge(t_free, g * NT + (t + 3))
                    if i == 0:
                        pe.wait_ge(v_staged, g * 2 + 2)
                        pe.wait_ge(o_free, g * (2 * NB) + (2 * b + 1))
                    kb = max(b - 1, 0) + i
                    last = i == len(TS[b]) - 1
                    mm = three(bank[OB][:, :], v_hi[:, kb], v_lo[:, kb], pt_hi[:, t % 2, :], pt_lo[:, t % 2, :],
                               i == 0, last)
                    if last:
                        mm.then_inc(pv_done, 1)

                def mod_sums():
                    pe.wait_ge(gemv_done, g * KT + 2 * KT)
                    pe.wait_ge(m_free, g * 2 + 2)
                    for f in range(KT):
                        mm = pe.matmul(bank[MB][:, 16 + f:17 + f], acc[:, f * P:(f + 1) * P], ones[:, 0:1],
                                       start=True, stop=True)
                    mm.then_inc(mod_done, 1)

                for slot in range(4 * NM):
                    if slot == 5:
                        square_sums()
                    for b in range(NB):
                        r = slot - 3 * b
                        if r == 12:
                            turn(b, 0)
                            turn(b, 1)
                        if r == 13:
                            values(b, 0)
                            if len(TS[b]) == 3:
                                turn(b, 2)
                            values(b, 1)
                        if r == 14 and len(TS[b]) == 3:
                            values(b, 2)
                    for b in range(NB):
                        if slot - 3 * b == 7:
                            scores(b, (0, 1))
                        if slot - 3 * b == 8:
                            scores(b, (2, 3))
                    if slot == 21:
                        mod_sums()
                    if slot % 2 == 0:
                        unit_waits(slot // 2)
                    unit_half(slot // 2, slot % 2)

            def pair(i, per, n, banks, rhs, k_wait=None, kn=8, k_off=0, first=True, last=True):
                pe.wait_ge(lo_ready, at(i, 2 * per, 2 * n + 2))
                for k in range(kn):
                    if k_wait is not None:
                        pe.wait_ge(k_wait, k + 1)
                    for u in range(2):
                        mm = three(bank[banks[u]][:, :], w_hi[:, n % 2, u, k, :], w_lo[:, n % 2, u, k, :],
                                   rhs[0][:, k_off + k, :], rhs[1][:, k_off + k, :],
                                   first and k == 0, last and k == kn - 1)
                        if k == kn - 1:
                            mm.then_inc(units_done, 1)

            pe.wait_ge(m_free, 2 * KV + 1)
            for n in range(D // PC):
                pair(None, 0, P_WO + n, (2 * n, 2 * n + 1), (h_hi, h_lo), m_lo if n == 0 else None)
            pe.wait_ge(sum_done, KT - 1)
            for b in range(NB):
                mm = pe.matmul(bank[0][:, b:b + 1], y_buf[:, 0, b * P:(b + 1) * P], ones[:, 0:1], start=True, stop=True)
            mm.then_inc(ss_done, 1)
            pe.wait_ge(diag_done, NB)
            pe.matmul(bank[1][:, :], ones[:, :], y_buf[:, 1, :], start=True, stop=True).then_inc(r_done, 1)

            with pe.Fori(0, FF // PC) as j:
                pe.wait_ge(a_free, j * 2 + 2)
                pair(j, 2, P_UP, (2, 3), (h_hi, h_lo), h2_ready)
                pe.wait_ge(b_free, j * 2 + 2)
                pair(j, 2, P_UP + 1, (4, 5), (h_hi, h_lo))

            with pe.Fori(0, 2) as i:
                def turn_out(q):
                    for u in range(2):
                        pe.wait_ge(ffn_tiles, i * 4 + (FT + 2 * q + u + 1))
                        pe.wait_ge(a_free, i * 4 + (2 + FT - 2 + 2 * q))
                        for b in range(NB):
                            mm = pe.transpose(bank[4 + 2 * q + u][:, b * P:(b + 1) * P],
                                              (a_buf, y_buf)[q][:, u, b * P:(b + 1) * P], ident[:, :])
                        mm.then_inc(yt_done, 1)

                for q in range(2):
                    for cc in range(3):
                        if cc == 0:
                            pe.wait_ge(ffn_tiles, i * 4 + (FT - 2 + 2 * q))
                        if cc == 2:
                            pe.wait_ge(ffn_tiles, FT)
                        pair(i, 6, P_DOWN + 3 * q + cc, (2 * q, 2 * q + 1), (g_hi, g_lo), kn=CH[cc], k_off=8 * cc,
                             first=cc == 0, last=cc == 2)
                        if q == 1 and cc == 0:
                            turn_out(0)
                turn_out(1)

        @block.vector
        def _(dve):
            steps = Tally(dve, dve_done)

            def rsqrt(i, per, n, cols, ss, scale, dst, fold=1.0):
                v, s, r, t = (st[:, m, 0:cols] for m in (1, 2, 3, 4))
                dve.tensor_scalar(v, ss, scale, EPS, MUL, ADD).then_inc(var_ready, 1)
                dve.wait_ge(root_ready, at(i, per, n + 1))
                steps.link(dve.reciprocal(r, s))
                steps.link(dve.tensor_tensor(t, r, r, MUL))
                steps.link(dve.tensor_tensor(t, t, v, MUL))
                steps.link(dve.tensor_scalar(t, t, -0.5 * fold, 1.5 * fold, MUL, ADD))
                steps.link(dve.tensor_tensor(dst, r, t, MUL))

            for u in range(2):
                dve.memset(pad_f[:, u * (S + 2):(u + 1) * (S + 2)], 0.0).then_inc(mix_free, 1)
            steps.link(dve.memset(half[:, :], 0.0))
            for a in range(2):
                dve.memset(half[a * HD:(a + 1) * HD, a:a + 1], 1.0).then_inc(half_done, 1)
            dve.wait_ge(const_done, 3)
            steps.link(dve.tensor_scalar(a_buf[:, 0, 0:BAND], ndist[:, :], -1.0, None, MUL))
            dve.tensor_tensor(ndist[:, :], ndist[:, :], a_buf[:, 0, 0:BAND], ALU.min).then_inc(dist_done, 1)
            dve.wait_ge(par_c, 3)
            steps.link(dve.scalar_tensor_tensor(c_act[:, 0, :], c_act[:, 1, :], 1.0, par[:, PA_C:PA_C + KT], ADD, MUL))
            steps.link(dve.tensor_scalar(c_act[:, 0, :], c_act[:, 0, :], 0.5, None, MUL))
            dve.wait_ge(x_sq, NB)
            rsqrt(None, 0, 0, NB, st[:, 0, 0:NB], 1.0 / D, st[:, 5, 0:NB])
            for b in range(NB):
                dve.tensor_scalar(xn[:, b, :], x_nat[:, b, :], st[:, 5, b:b + 1], None, MUL).then_inc(x_n, 1)
            for k in range(KT):
                dve.wait_ge(ada0_in[k % 4], 16 * (k // 4) + 16)
                if k == 0:
                    ins = dve.tensor_scalar(acc0[:, :], ada0[:, 0, :], c_act[:, 0, 0:1], None, MUL)
                else:
                    dve.wait_ge(gemv_done, k)
                    ins = dve.scalar_tensor_tensor(acc0[:, :], ada0[:, k % 4, :], c_act[:, 0, k:k + 1], acc0[:, :],
                                                   MUL, ADD)
                ins.then_inc(gemv_done, 1)
            dve.wait_ge(mod_done, 1)
            steps.link(dve.tensor_tensor(mod[:, 0:2 * KT], bank[6][:, 0:2 * KT], par[:, PA_B:PA_B + 2 * KT], ADD))
            steps.link(dve.scalar_tensor_tensor(amp[:, 0, :], mod[:, KT:2 * KT], 1.0, par[:, PA_G1:PA_G1 + KT],
                                                ADD, MUL))
            dve.wait_ge(xt_out, 2 * KT)

            def h_low(k):
                dve.wait_ge(h_h, k + 1)
                dve.tensor_tensor(h_lo[:, k, :], hT[:, k, :], h_hi[:, k, :], SUB).then_inc(h_ready, 1)

            for k in range(KT):
                dve.tensor_scalar(hT[:, k, :], hT[:, k, :], amp[:, 0, k:k + 1], mod[:, k:k + 1],
                                  MUL, ADD).then_inc(h_f, 1)
                if k >= 1:
                    h_low(k - 1)
            h_low(KT - 1)

            dve.wait_ge(g_act, NB)
            steps.link(dve.tensor_tensor(k_sq, k_nat, k_nat, MUL))
            steps.link(dve.tensor_reduce(st[:, 0, :], k_sq.rearrange("p (a d) -> p a d", d=HD), AX.X, ADD))
            rsqrt(None, 0, 1, NB * KV, st[:, 0, 0:NB * KV], 1.0 / HD, st[:, 6, :])
            dve.tensor_tensor(k_nat.rearrange("p (a d) -> p a d", d=HD), k_nat.rearrange("p (a d) -> p a d", d=HD),
                              st[:, 6, :].unsqueeze(2).to_broadcast([P, NB * KV, HD]), MUL).then_inc(kn_ready, 1)
            dve.wait_ge(units_done, 4)
            for b, done in ((0, t_free), (1, t_free), (3, m_free)):
                dve.tensor_copy(v_nat[:, b, :], bank[4 + b][:, 0:PC]).then_inc(done, 1)
            for f in range(2):
                dve.wait_ge(kt_done, f + 1)
                dve.tensor_scalar(k_T[:, f, :], bank[SC[f]][:, :], par[:, PA_KG:PA_KG + 1], par[:, PA_QG:PA_QG + 1],
                                  MUL, MUL).then_inc(score_free, 1)
            dve.wait_ge(score_free, 2)
            for j in range(KV):
                a = (j % 2) * HD
                dve.wait_ge(kh_done, 2 * j + 2)
                for o in range(2):
                    dve.tensor_tensor(k_st[o * HD:(o + 1) * HD, 1, j, :], k_T[a:a + HD, j // 2, :],
                                      k_st[a:a + HD, 0, j, :], SUB).then_inc(kl_done, 1)
            dve.wait_ge(o_free, 1)
            dve.wait_ge(m_free, 1)
            dve.wait_ge(t_free, 2)
            dve.wait_ge(kl_done, 2 * KV)
            dve.wait_ge(sink_in, 16)

            with dve.Fori(0, KV) as g:
                steps.enter(g, STEPS)

                def gemv(k):
                    dve.wait_ge(ada_in[k % 2], g * (8 * KT) + (16 * (k // 2) + 16))
                    if k == 0:
                        ins = dve.tensor_scalar(acc[:, :], ada[:, 0, :], c_act[:, 0, 0:1], None, MUL)
                    else:
                        dve.wait_ge(gemv_done, g * KT + (KT + k))
                        ins = dve.scalar_tensor_tensor(acc[:, :], ada[:, k % 2, :], c_act[:, 0, k:k + 1], acc[:, :],
                                                       MUL, ADD)
                    ins.then_inc(gemv_done, 1)

                def stage_values():
                    v = v_nat[:, :, bass.ds(g * HD, HD)]
                    for o in range(2):
                        steps.inc(dve.tensor_scalar(v_hi[:, :, o, :], v, 1.0, None, MUL))
                    dve.wait_ge(dve_done, steps.turn + steps.n)
                    for o in range(2):
                        dve.tensor_tensor(v_lo[:, :, o, :], v, v_hi[:, :, o, :], SUB).then_inc(v_staged, 1)

                def query_low(u):
                    dve.wait_ge(q_hi, g * HG + (2 * u + 2))
                    for o in range(2):
                        r, w = slice(o * HD, (o + 1) * HD), slice((1 - o) * HD, (2 - o) * HD)
                        dve.tensor_tensor(q_st[w, 2 * u + o, :], y_buf[r, u, :], q_st[r, 2 * u + o, :],
                                          SUB).then_inc(q_lo, 1)

                def query_norm():
                    dve.wait_ge(ssq_done, g + 1)
                    rsqrt(g, 1, 2, NB * HG, bank[MB][:, 0:NB * HG], 1.0 / HD, st[:, 7, :], RS)
                    dve.tensor_copy(sm[:, 6, :, :].rearrange("p b h -> p (b h)"), st[:, 7, :]).then_inc(m_free, 1)
                    dve.wait_ge(m_free, g * 2 + 2)

                def take(b, hs):
                    w = P * len(TS[b])
                    c0 = P if b == 0 else 0
                    for h in hs:
                        dve.wait_ge(s_done, g * (NB * HG) + (b * HG + h + 1))
                        if b == 0 and h == 0:
                            dve.wait_ge(bias_done, g + HG)
                        dve.scalar_tensor_tensor(prob[:, b % 2, h, 0:w], bank[SC[h % 2]][:, 0:w], sm[:, 6, b, h:h + 1],
                                                 bias[:, h, c0:c0 + w], MUL, ADD).then_inc(score_free, 1)

                def shift(b):
                    w = P * len(TS[b])
                    dve.wait_ge(score_free, g * (NB * HG) + (b * HG + HG + 2))
                    steps.link(dve.tensor_reduce(sm[:, 0, b, :], prob[:, b % 2, :, 0:w], AX.X, MAX))
                    steps.link(dve.tensor_tensor(sm[:, 0, b, :], sm[:, 0, b, :], sink_b[:, bass.ds(g * HG, HG)], MAX))
                    steps.link(dve.tensor_scalar(sm[:, 1, b, :], sm[:, 0, b, :], -1.0, None, MUL))
                    dve.tensor_tensor(sm[:, 2, b, :], sm[:, 1, b, :], sink_b[:, bass.ds(g * HG, HG)],
                                      ADD).then_inc(shift_ready, 1)

                def normalise(b):
                    w = P * len(TS[b])
                    dve.wait_ge(exp_done, g * (NB * (HG + 1)) + (b + 1) * (HG + 1))
                    steps.link(dve.tensor_tensor(sm[:, 5, b, :], sm[:, 3, b, :], sm[:, 4, b, :], ADD))
                    steps.link(dve.reciprocal(sm[:, 5, b, :], sm[:, 5, b, :]))
                    for h in range(HG):
                        dve.tensor_scalar(prob[:, b % 2, h, 0:w], prob[:, b % 2, h, 0:w], sm[:, 5, b, h:h + 1], None,
                                          MUL).then_inc(p_ready, 1)

                def turned_low(ts):
                    for t in ts:
                        dve.wait_ge(pt_h, g * NT + (t + 1))
                        dve.tensor_tensor(pt_lo[:, t % 2, :], bank[TB[t % 2]][:, :], pt_hi[:, t % 2, :],
                                          SUB).then_inc(t_free, 1)

                def conv_in(u):
                    dve.wait_ge(units_done, g * (2 * NM) + (2 * P_MIX + 4 + u + 1))
                    dve.wait_ge(g_act, g * 8 + (NB + 3 + u))
                    dve.tensor_tensor(pad[u][:, 1:S + 1], bank[u][:, :], a_buf[:, u, :], MUL).then_inc(g_dve, 1)

                def taps(u):
                    def w(tap):
                        return par[:, bass.ds(g * 2 + (PA_CW + tap * KT + u), 1)]
                    dve.wait_ge(g_dve, g * 4 + (u + 1))
                    steps.link(dve.tensor_scalar(a_buf[:, u, :], pad[u][:, 0:S], w(0), None, MUL))
                    for tap in (1, 2):
                        steps.link(dve.scalar_tensor_tensor(a_buf[:, u, :], pad[u][:, tap:tap + S], w(tap),
                                                            a_buf[:, u, :], MUL, ADD))

                def conv_out(u):
                    dve.wait_ge(units_done, g * (2 * NM) + (2 * P_MIX + 6 + u + 1))
                    dve.tensor_tensor(a_buf[:, u, :], bank[u][:, :], a_buf[:, u, :], MUL).then_inc(g_dve, 1)

                def gate_a(u):
                    dve.wait_ge(g_dve, g * 4 + (u + 3))
                    dve.wait_ge(g_act, g * 8 + (NB + 5 + u))
                    dve.scalar_tensor_tensor(a_buf[:, u, :], b_buf[:, u, :], 1.0, a_buf[:, u, :],
                                             ADD, MUL).then_inc(ma_done, 1)

                def merge(u):
                    dve.wait_ge(g_act, g * 8 + (NB + 7 + u))
                    dve.wait_ge(ma_done, g * 2 + (u + 1))
                    steps.link(dve.scalar_tensor_tensor(b_buf[:, u, :], b_buf[:, u, :], 1.0, y_buf[:, u, :], ADD, MUL))
                    dve.tensor_tensor(merged[:, bass.ds(g * 2 + u, 1), :].rearrange("p a n -> p (a n)"),
                                      b_buf[:, u, :], a_buf[:, u, :], ADD).then_inc(mix_free, 1)

                gemv(0)
                gemv(1)
                stage_values()
                query_low(0)
                query_low(1)
                gemv(2)
                query_norm()
                take(0, (0, 1))
                take(0, (2, 3))
                shift(0)
                gemv(3)
                conv_in(0)
                take(1, (0, 1))
                normalise(0)
                take(1, (2, 3))
                shift(1)
                conv_in(1)
                turned_low(TS[0])
                taps(0)
                normalise(1)
                take(2, (0, 1))
                taps(1)
                conv_out(0)
                take(2, (2, 3))
                shift(2)
                turned_low(TS[1])
                conv_out(1)
                take(3, (0, 1))
                normalise(2)
                gemv(4)
                take(3, (2, 3))
                shift(3)
                gate_a(0)
                turned_low(TS[2])
                gemv(5)
                normalise(3)
                gate_a(1)
                gemv(6)
                gemv(7)
                turned_low(TS[3])
                dve.wait_ge(mod_done, g + 2)
                dve.tensor_tensor(mod[:, bass.ds(g * KT + 2 * KT, KT)], bank[MB][:, 16:16 + KT],
                                  par[:, bass.ds(g * KT + (PA_B + 2 * KT), KT)], ADD).then_inc(m_free, 1)
                dve.wait_ge(o_free, g * (2 * NB) + (2 * NB + 1))
                merge(0)
                merge(1)
                steps.leave(KV)

            dve.wait_ge(m_free, 2 * KV + 1)
            steps.link(dve.scalar_tensor_tensor(amp[:, 1, :], mod[:, 4 * KT:5 * KT], 1.0, par[:, PA_G2:PA_G2 + KT],
                                                ADD, MUL))
            dve.wait_ge(mix_free, 2 * KV + 2)
            for k in range(KT):
                dve.wait_ge(m_hi, k + 1)
                dve.scalar_tensor_tensor(h_lo[:, k, :], merged[:, k, :], 0.5, h_hi[:, k, :], MUL, SUB).then_inc(m_lo, 1)
            for f in range(KT):
                dve.wait_ge(units_done, 2 * P_WO + f + 1)
                dve.scalar_tensor_tensor(xT[:, f, :], bank[f][:, :], mod[:, 2 * KT + f:2 * KT + f + 1], xT[:, f, :],
                                         MUL, ADD).then_inc(b_free if f in (4, 5) else x2_done, 1)
                if f >= 1:
                    g_ = f - 1
                    if g_ in (2, 3):
                        dve.wait_ge(a_free, g_ - 1)
                    else:
                        dve.wait_ge(x2_sq, g_ + 1 if g_ < 2 else g_ - 1)
                    square_add(dve, g_, sum_done, y_buf, b_buf, ADD)
            dve.wait_ge(x2_sq, KT - 2)
            square_add(dve, KT - 1, sum_done, y_buf, b_buf, ADD)
            dve.wait_ge(ss_done, 1)
            rsqrt(None, 0, 2 + KV, NB, bank[0][:, 0:NB], 1.0 / D, st[:, 5, 0:NB])
            for b in range(NB):
                dve.tensor_scalar(y_buf[:, 1, b * P:(b + 1) * P], ident[:, :], st[:, 5, b:b + 1], None,
                                  MUL).then_inc(diag_done, 1)
            dve.wait_ge(r_done, 1)

            def h2_low(f):
                dve.wait_ge(h2_h, f + 1)
                dve.scalar_tensor_tensor(h_lo[:, f, :], a_buf[:, f % 2, :], mod[:, 3 * KT + f:3 * KT + f + 1],
                                         h_hi[:, f, :], ADD, SUB).then_inc(h2_ready, 1)

            for f in range(KT):
                if f >= 2:
                    dve.wait_ge(h2_ready, f - 1)
                dve.scalar_tensor_tensor(a_buf[:, f % 2, :], xT[:, f, :], amp[:, 1, f:f + 1], bank[1][:, :],
                                         MUL, MUL).then_inc(t2_done, 1)
                if f >= 1:
                    h2_low(f - 1)
            h2_low(KT - 1)

            with dve.Fori(0, FF // PC) as j:
                steps.enter(j, STEPS_UP)
                for u in range(2):
                    def w(row):
                        return par[:, bass.ds(j * 2 + (row + u), 1)]
                    dve.wait_ge(a_free, j * 2 + (2 + u + 1))
                    steps.link(dve.tensor_scalar(a_buf[:, u, :], pad[u][:, 0:S], w(PA_FW), w(PA_FB), MUL, ADD))
                    steps.link(dve.scalar_tensor_tensor(a_buf[:, u, :], pad[u][:, 1:S + 1], w(PA_FW + FT),
                                                        a_buf[:, u, :], MUL, ADD))
                    dve.scalar_tensor_tensor(a_buf[:, u, :], pad[u][:, 2:S + 2], w(PA_FW + 2 * FT), a_buf[:, u, :],
                                             MUL, ADD).then_inc(conv_done, 1)
                for u in range(2):
                    dve.wait_ge(f_sq, j * 2 + (u + 1))
                    dve.scalar_tensor_tensor(b_buf[:, u, :], b_buf[:, u, :], 1.0 / GELU_C, a_buf[:, u, :],
                                             ADD, MUL).then_inc(z_done, 1)
                for u in range(2):
                    dve.wait_ge(f_th, j * 2 + (u + 1))
                    steps.link(dve.scalar_tensor_tensor(y_buf[:, u, :], b_buf[:, u, :], 1.0, a_buf[:, u, :], ADD, MUL))
                for u in range(2):
                    dve.wait_ge(units_done, j * 4 + (2 * P_UP + 2 + u + 1))
                    dve.scalar_tensor_tensor(y_buf[:, u, :], bank[4 + u][:, :], 0.5, y_buf[:, u, :],
                                             MUL, MUL).then_inc(b_free, 1)
                for u in range(2):
                    hi = g_hi[:, bass.ds(j * 2 + u, 1), :].rearrange("p a n -> p (a n)")
                    lo = g_lo[:, bass.ds(j * 2 + u, 1), :].rearrange("p a n -> p (a n)")
                    dve.wait_ge(b_free, j * 2 + (2 + u + 1))
                    steps.link(dve.tensor_scalar(hi, y_buf[:, u, :], 1.0, None, MUL))
                    dve.tensor_tensor(lo, y_buf[:, u, :], hi, SUB).then_inc(ffn_tiles, 1)
                steps.leave(FF // PC)

            with dve.Fori(0, 2) as i:
                for q in range(2):
                    for u in range(2):
                        f = 2 * q + u
                        dve.wait_ge(units_done, i * 12 + (2 * P_DOWN + 6 * q + 4 + u + 1))
                        dve.scalar_tensor_tensor((a_buf, y_buf)[q][:, u, :], bank[2 * q + u][:, :],
                                                 mod[:, bass.ds(i * 4 + (5 * KT + f), 1)],
                                                 xT[:, bass.ds(i * 4 + f, 1), :].rearrange("p a n -> p (a n)"),
                                                 MUL, ADD).then_inc(ffn_tiles, 1)


def square_add(dve, f, sum_done, y_buf, b_buf, ADD):
    if f == 0:
        return
    if f == 1:
        ins = dve.tensor_tensor(y_buf[:, 0, :], b_buf[:, 0, :], b_buf[:, 1, :], ADD)
    else:
        dve.wait_ge(sum_done, f - 1)
        ins = dve.tensor_tensor(y_buf[:, 0, :], y_buf[:, 0, :], b_buf[:, f % 2, :], ADD)
    ins.then_inc(sum_done, 1)


_INS = ["x", "c", "w_ada", "b_ada", "norm1_gain", "w_in", "conv_w", "q_gain", "k_gain", "sink", "w_o",
        "norm2_gain", "w_up", "ffn_conv_w", "ffn_conv_b", "w_down"]


def kernel(**inputs):
    import numpy as _np
    import concourse.bacc as _bacc
    from concourse import mybir as _mybir
    from concourse.bass_utils import run_bass_kernel_spmd as _run

    nc = _bacc.Bacc("TRN2", target_bir_lowering=False, num_devices=1)
    arrays, args = {}, []
    for name in _INS:
        a = _np.ascontiguousarray(inputs[name])
        arrays[f"in_{name}_dram"] = a
        args.append(nc.dram_tensor(f"in_{name}_dram", a.shape, _mybir.dt.from_np(a.dtype), kind="ExternalInput").ap())
    shape = inputs["x"].shape
    out = nc.dram_tensor("out_0_dram", shape, _mybir.dt.float32, kind="ExternalOutput").ap()
    encoder_block(nc, *args, out)
    r = _run(nc, [arrays], core_ids=[0])
    return r.results[0]["out_0_dram"]
```

```python
import concourse.bass as bass
from concourse import mybir
from contextlib import ExitStack
import numpy as np


class Tally:

    def __init__(self, eng, sem):
        self.eng, self.sem, self.n, self.turn = eng, sem, 0, 0

    def enter(self, i, per):
        self.start, self.per, self.turn = self.n, per, i * per

    def leave(self, turns):
        assert self.n - self.start == self.per, (self.n - self.start, self.per)
        self.n, self.turn = self.start + turns * self.per, 0

    def inc(self, ins):
        ins.then_inc(self.sem, 1)
        self.n += 1

    def link(self, ins):
        self.inc(ins)
        self.eng.wait_ge(self.sem, self.turn + self.n)


def encoder_block(nc, x, c, w_ada, b_ada, norm1_gain, w_in, conv_w, q_gain, k_gain, sink, w_o,
                  norm2_gain, w_up, ffn_conv_w, ffn_conv_b, w_down, out):
    fp32, f32r = mybir.dt.float32, mybir.dt.float32r
    ALU, ACT, AX = mybir.AluOpType, mybir.ActivationFunctionType, mybir.AxisListType
    MUL, ADD, SUB, MAX = ALU.mult, ALU.add, ALU.subtract, ALU.max

    P = 128
    S, D = x.shape[1], x.shape[2]
    KT = D // P
    NB = S // P
    HD = q_gain.shape[1]
    H = D // HD
    KV = H // 4
    HG = H // KV
    FF = w_down.shape[1]
    FT = FF // P
    PC = 2 * P
    EPS = 1e-6
    BAND = 3 * P
    MASKED = -1e35
    GELU_C, GELU_S = 0.044715, float(np.sqrt(2 / np.pi))
    RS = 1.0 / np.sqrt(HD)

    COL_B, COL_C, COL_U, COL_Q = 0, D, 2 * D, 3 * D
    COL_K = 4 * D
    COL_V = COL_K + KV * HD
    COL_GA = COL_V + KV * HD
    COL_GB = COL_GA + D
    MIX = [COL_Q, COL_C, COL_U, COL_B, COL_GA, COL_GB]
    NM = len(MIX)

    P_MIX = 2
    P_WO = P_MIX + NM * KV
    P_UP = P_WO + D // PC
    P_DOWN = P_UP + 2 * (FF // PC)
    CH = [8, 8, FT - 16]
    P_END = P_DOWN + len(CH) * (D // PC)

    PA_C, PA_B, PA_G1, PA_G2, PA_CW = 0, KT, 7 * KT, 8 * KT, 9 * KT
    PA_QG, PA_KG = 12 * KT, 12 * KT + 1
    ROWS1 = 12 * KT + 2
    PA_FW, PA_FB = ROWS1, ROWS1 + 3 * FT
    ROWS2 = 4 * FT
    HT = KT // 2
    RING = 8

    def k_rows(w):
        return w[0].rearrange("(k p) n -> p k n", p=P)

    wi, wo, wu, wd = k_rows(w_in), k_rows(w_o), k_rows(w_up), k_rows(w_down)
    out_v = out[0].rearrange("(b p) n -> p b n", p=P)

    ctx = ExitStack()
    with ctx:
        def sb(name, shape, dt=fp32, into=ctx):
            return into.enter_context(nc.sbuf_tensor(name, shape, dt))

        def sem(name):
            return ctx.enter_context(nc.semaphore(name))

        h_hi = sb("h_hi", [P, KT, S], f32r)
        h_lo = sb("h_lo", [P, KT, S], f32r)
        xT = sb("xT", [P, KT, S])
        w_raw = sb("w_raw", [P, 2, 8, PC])
        w_hi = sb("w_hi", [P, 2, 2, 8, P], f32r)
        w_lo = sb("w_lo", [P, 2, 2, 8, P], f32r)
        par = sb("par", [P, ROWS1 + ROWS2])
        mod = sb("mod", [P, 6 * KT])
        amp = sb("amp", [P, 2, KT])
        c_act = sb("c_act", [P, 2, KT])
        ident = sb("ident", [P, P])
        ones = sb("ones", [P, P])
        sink_b = sb("sink_b", [P, H])
        ndist = sb("ndist", [P, BAND])
        st = sb("st", [P, 8, 16])
        sm = sb("sm", [P, 7, NB, HG])
        a_buf = sb("a_buf", [P, 2, S])
        b_buf = sb("b_buf", [P, 2, S])
        y_buf = sb("y_buf", [P, 2, S])
        pad_f = sb("pad_f", [P, 2 * (S + 2)])
        pad = [pad_f[:, u * (S + 2):(u + 1) * (S + 2)] for u in range(2)]

        start = ExitStack()
        x_nat = sb("x_nat", [P, NB, D], into=start)
        hT = sb("hT", [P, KT, S], into=start)
        ada0 = sb("ada0", [P, RING, 2, D // 2], into=start)
        acc0 = sb("acc0", [P, 2, 2, D // 2], into=start)
        start.close()

        mixer = ExitStack()
        merged = sb("merged", [P, KT, S], into=mixer)
        k_st = sb("k_st", [P, 2, KV, S], f32r, into=mixer)
        v_nat = sb("v_nat", [P, NB, KV * HD], into=mixer)
        q_st = sb("q_st", [P, HG, S], f32r, into=mixer)
        v_hi = sb("v_hi", [P, NB, 2, HD], f32r, into=mixer)
        v_lo = sb("v_lo", [P, NB, 2, HD], f32r, into=mixer)
        bias = sb("bias", [P, HG, BAND], into=mixer)
        prob = sb("prob", [P, 2, HG, BAND], into=mixer)
        pt_hi = sb("pt_hi", [P, 2, HG * P], f32r, into=mixer)
        pt_lo = sb("pt_lo", [P, 2, HG * P], f32r, into=mixer)
        ada = sb("ada", [P, 2, D], into=mixer)
        acc = sb("acc", [P, D], into=mixer)
        mixer.close()
        k_nat = prob[:, 0, :, :].rearrange("p h j -> p (h j)")[:, 0:NB * KV * HD]
        k_sq = prob[:, 1, :, :].rearrange("p h j -> p (h j)")[:, 0:NB * KV * HD]
        k_T = merged[:, 0:2, :]

        channel = ExitStack()
        g_hi = sb("g_hi", [P, FT, S], f32r, into=channel)
        g_lo = sb("g_lo", [P, FT, S], f32r, into=channel)
        channel.close()
        par_rows = w_raw[:, 1, :, :].rearrange("p k n -> p (k n)")

        bank = [ctx.enter_context(nc.psum_tensor(f"bank{i}", [P, S], fp32)) for i in range(8)]
        SC, TB, OB, MB = (2, 3), (4, 5), 6, 7

        par_in, sink_in = sem("par_in"), sem("sink_in")
        c_in = sem("c_in")
        x_in = [sem(f"x_in{b}") for b in range(NB)]
        ada0_in = [sem(f"ada0_in{k}") for k in range(RING)]
        ada_in = [sem(f"ada_in{k}") for k in range(2)]
        w_in_slot = [sem(f"w_loaded{s}") for s in range(2)]
        out_dma = [sem(f"out_stored{s}") for s in range(2)]
        const_done = sem("const_done")
        dist_done = sem("dist_done")
        bias_done = sem("bias_done")
        hi_ready = sem("hi_ready")
        lo_ready = sem("lo_ready")
        units_done = sem("units_done")
        par_t, par_c = sem("par_transposed"), sem("par_copied")
        c_t, c_th = sem("c_transposed"), sem("c_tanh")
        x_sq = sem("x_squared")
        xd_done, xr_done = sem("x_diag"), sem("x_rstd_spread")
        xt_done, xt_out = sem("x_transposed"), sem("xt_copied")
        gemv_done, mod_done = sem("gemv_done"), sem("mod_summed")
        h_f, h_h, h_ready = sem("h_float"), sem("h_high"), sem("h_ready")
        var_ready, root_ready = sem("var_ready"), sem("root_ready")
        kn_ready, kt_done, kh_done, kl_done = sem("k_normed"), sem("k_transposed"), sem("k_high"), sem("k_low")
        g_act, g_dve = sem("drained_by_act"), sem("drained_by_dve")
        score_free, t_free, o_free, m_free = sem("score_free"), sem("t_free"), sem("o_free"), sem("m_free")
        mix_free = sem("mix_free")
        q_sq, q_hi, q_lo = sem("q_squared"), sem("q_high"), sem("q_low")
        ssq_done, s_done, t_done, pt_h, pv_done = (sem("q_sums"), sem("scores"), sem("p_transposed"),
                                                   sem("pt_high"), sem("pv"))
        v_staged, shift_ready, exp_done, p_ready = sem("v_staged"), sem("shift_ready"), sem("exp_done"), sem("p_ready")
        ma_done = sem("branch_a_gated")
        m_hi, m_lo, m_lo_dve = sem("merged_high"), sem("merged_low"), sem("merged_low_last")
        x2_done, x2_sq, sum_done, ss_done, diag_done, r_done = (sem("x2"), sem("x2_squared"), sem("x2_summed"),
                                                                sem("norm2_sums"), sem("diag"), sem("rstd_spread"))
        t2_done, h2_h, h2_ready = sem("h2_scaled"), sem("h2_high"), sem("h2_ready")
        a_free, b_free = sem("act_drained_ffn"), sem("dve_drained_ffn")
        conv_done, f_sq, z_done, f_th = sem("ffn_conv"), sem("ffn_squared"), sem("gelu_arg"), sem("gelu_tanh")
        ffn_tiles = sem("ffn_tiles")
        yt_done = sem("y_transposed")
        act_done, dve_done, pool_done = sem("act_steps"), sem("dve_steps"), sem("pool_steps")

        def at(i, per, n):
            return n if i is None else i * per + n

        TS = [[0, 1], [2, 3, 4], [5, 6, 7], [8, 9]]
        NT = 10
        STEPS, STEPS_UP = 38, 8

        block = ctx.enter_context(nc.Block())

        @block.sync
        def _(sp):
            def load(i, per, n, src):
                if n >= 2:
                    sp.wait_ge(lo_ready, at(i, 2 * per, 2 * n - 2))
                sp.dma_start(w_raw[:, n % 2, 0:src.shape[1], :], src).then_inc(w_in_slot[n % 2], 16)

            sp.dma_start(par_rows[0:KT, 0:P], c.rearrange("a (f p) -> (a f) p", p=P)).then_inc(c_in, 16)
            for b in range(NB):
                sp.dma_start(x_nat[:, b, :], x[0, b * P:(b + 1) * P, :]).then_inc(x_in[b], 16)
            for n in range(2 * KT):
                a, k = n // KT, n % KT
                if n >= RING:
                    sp.wait_ge(gemv_done, n - RING + 1)
                sp.dma_start(ada0[:, n % RING],
                             w_ada[0, k * P:(k + 1) * P, 0:2 * D].rearrange("p (s n) -> p s n", s=2)[
                                 :, :, a * (D // 2):(a + 1) * (D // 2)]).then_inc(ada0_in[n % RING], 16)
                if n == 5:
                    load(None, 0, 0, wi[:, :, COL_K:COL_K + PC])
            sp.wait_ge(par_t, 2)
            load(None, 0, 1, wi[:, :, COL_V:COL_V + PC])
            with sp.Fori(1, KV + 1) as g1:
                g = g1 - 1
                for n in range(NM):
                    load(g, NM, P_MIX + n, wi[:, :, bass.ds(g1 * PC + (MIX[n] - PC), PC)])
                    for k in ([], [], [0, 1, 2, 3], [4, 5, 6], [7], [])[n]:
                        sp.wait_ge(gemv_done, g * KT + (2 * KT + k - 1))
                        sp.dma_start(ada[:, k % 2, :],
                                     w_ada[0, k * P:(k + 1) * P, bass.ds(g1 * D + D, D)]).then_inc(ada_in[k % 2], 16)
            for n in range(D // PC):
                load(None, 0, P_WO + n, wo[:, :, n * PC:(n + 1) * PC])
            with sp.Fori(1, FF // PC + 1) as j1:
                j = j1 - 1
                for n in range(2):
                    load(j, 2, P_UP + n, wu[:, :, bass.ds(j1 * PC + (n * FF - PC), PC)])
            with sp.Fori(1, 3) as i1:
                i = i1 - 1
                for n in range(6):
                    q, k0 = n // 3, 8 * (n % 3)
                    load(i, 6, P_DOWN + n, wd[:, k0:k0 + CH[n % 3], bass.ds(i1 * (2 * PC) + (q - 2) * PC, PC)])

        @block.gpsimd
        def _(pool):
            steps = Tally(pool, pool_done)

            def low(i, per, n):
                for u in range(2):
                    pool.wait_ge(hi_ready, at(i, 2 * per, 2 * n + u + 1))
                    pool.tensor_tensor(w_lo[:, n % 2, u], w_raw[:, n % 2, :, u * P:(u + 1) * P],
                                       w_hi[:, n % 2, u], SUB).then_inc(lo_ready, 1)

            steps.link(pool.memset(ident[:, :], 0.0))
            pool.affine_select(out=ident[:, :], in_=ident[:, :], compare_op=ALU.not_equal, fill=1.0, base=0,
                               pattern=[[-1, P]], channel_multiplier=1).then_inc(const_done, 1)
            pool.memset(ones[:, :], 1.0).then_inc(const_done, 1)
            pool.iota(ndist[:, :], pattern=[[-1, BAND]], base=P, channel_multiplier=1,
                      allow_small_or_imprecise_dtypes=True).then_inc(const_done, 1)
            pool.wait_ge(dist_done, 1)
            steps.link(pool.affine_select(out=ndist[:, :], in_=ndist[:, :], compare_op=ALU.is_ge, fill=MASKED,
                                          base=2 * P, pattern=[[-1, BAND]], channel_multiplier=1))
            steps.link(pool.affine_select(out=ndist[:, :], in_=ndist[:, :], compare_op=ALU.is_ge, fill=MASKED,
                                          base=0, pattern=[[1, BAND]], channel_multiplier=-1))
            low(None, 0, 0)
            low(None, 0, 1)
            pool.wait_ge(h_ready, KT)
            for h in range(HG):
                slope = float(np.float32(2.0 ** (-8.0 * (h + 1) / H)))
                pool.tensor_scalar(bias[:, h, :], ndist[:, :], slope, 1.0, MUL, MUL).then_inc(bias_done, 1)
            low(None, 0, 2)
            with pool.Fori(0, KV) as g:
                for n in range(NM):
                    if n == 5:
                        pool.wait_ge(score_free, g * (NB * HG) + (NB * HG + 2))
                    low(g, NM, P_MIX + n + 1)
                    if n == 5:
                        pool.tensor_scalar(bias[:, :, :], bias[:, :, :], 2.0 ** (-8 * HG // H), 1.0,
                                           MUL, MUL).then_inc(bias_done, 1)
            for k in range(KT - 2):
                pool.wait_ge(m_hi, k + 1)
                pool.tensor_tensor(h_lo[:, k, :], merged[:, k, :], h_hi[:, k, :], SUB).then_inc(m_lo, 1)
            for n in range(P_WO + 1, P_UP + 2):
                low(None, 0, n)
            with pool.Fori(0, FF // PC) as j:
                for n in range(2):
                    low(j, 2, P_UP + n + 2)
            for n in range(P_DOWN + 2, P_END):
                low(None, 0, n)

        @block.scalar
        def _(act):
            steps = Tally(act, act_done)

            def high(i, per, n, units=(0, 1)):
                act.wait_ge(w_in_slot[n % 2], at(i, 16 * per // 2, 16 * (n // 2) + 16))
                if n >= 2:
                    act.wait_ge(units_done, at(i, 2 * per, 2 * n - 2))
                for u in units:
                    act.activation(w_hi[:, n % 2, u], w_raw[:, n % 2, :, u * P:(u + 1) * P],
                                   ACT.Copy).then_inc(hi_ready, 1)

            rows = KT
            for src, n in ((b_ada, 6 * KT), (norm1_gain, KT), (norm2_gain, KT), (conv_w[0], 3 * KT)):
                act.dma_start(par_rows[rows:rows + n, 0:P],
                              src.rearrange("a (f p) -> (a f) p", p=P)).then_inc(par_in, 16)
                rows += n
            for r, src in enumerate((q_gain, k_gain)):
                for a in range(2):
                    act.dma_start(par_rows[rows + r:rows + r + 1, a * HD:(a + 1) * HD], src).then_inc(par_in, 16)
            act.dma_start(par_rows[0:3 * FT, P:2 * P],
                          ffn_conv_w[0].rearrange("a (f p) -> (a f) p", p=P)).then_inc(par_in, 16)
            act.dma_start(par_rows[3 * FT:4 * FT, P:2 * P],
                          ffn_conv_b.rearrange("a (f p) -> (a f) p", p=P)).then_inc(par_in, 16)
            act.dma_start(sink_b[:, :], sink.to_broadcast([P, H])).then_inc(sink_in, 16)

            act.wait_ge(c_t, 1)
            act.activation(c_act[:, 1, :], bank[5][:, 0:KT], ACT.Tanh, scale=0.5).then_inc(c_th, 1)
            for b in range(NB):
                act.wait_ge(x_in[b], 16)
                act.activation(hT[:, 2 * b:2 * b + 2, :].rearrange("p k n -> p (k n)"), x_nat[:, b, :], ACT.Square,
                               accum_out=st[:, 0, b:b + 1]).then_inc(x_sq, 1)
            roots = 0

            def root(i, per, n, cols, src, dst):
                act.wait_ge(var_ready, at(i, per, n + 1))
                act.activation(st[:, dst, 0:cols], st[:, src, 0:cols], ACT.Sqrt).then_inc(root_ready, 1)

            root(None, 0, 0, NB, 1, 2)
            for m in range(KT):
                act.wait_ge(xt_done, m + 1)
                act.activation(xT[:, m, :], bank[m % 4][:, :], ACT.Copy).then_inc(xt_out, 1)
            for t, (r0, n) in enumerate(((0, ROWS1), (ROWS1, ROWS2))):
                act.wait_ge(par_t, t + 1)
                act.activation(par[:, r0:r0 + n], bank[6 + t][:, 0:n], ACT.Copy).then_inc(par_c, 1)
            high(None, 0, 0)
            for k in range(KT):
                act.wait_ge(h_f, k + 1)
                act.activation(h_hi[:, k, :], hT[:, k, :], ACT.Copy).then_inc(h_h, 1)
            high(None, 0, 1)
            act.wait_ge(units_done, 2)
            act.wait_ge(h_ready, KT)
            for b in range(NB):
                act.activation(k_nat[:, b * PC:(b + 1) * PC], bank[b][:, 0:PC], ACT.Copy).then_inc(g_act, 1)
            high(None, 0, 2)
            root(None, 0, 1, NB * KV, 1, 2)
            act.wait_ge(units_done, 4)
            act.activation(v_nat[:, 2, :], bank[6][:, 0:PC], ACT.Copy).then_inc(o_free, 1)
            for j in range(KV):
                act.wait_ge(score_free, j // 2 + 1)
                a = (j % 2) * HD
                for o in range(2):
                    act.activation(k_st[o * HD:(o + 1) * HD, 0, j, :], k_T[a:a + HD, j // 2, :],
                                   ACT.Copy).then_inc(kh_done, 1)

            with act.Fori(0, KV) as g:
                U = 2 * P_MIX

                def unit(n):
                    act.wait_ge(units_done, g * (2 * NM) + (U + n + 1))

                def query(u):
                    unit(u)
                    act.wait_ge(mix_free, g * 2 + 2)
                    act.activation(y_buf[:, u, :], bank[u][:, :], ACT.Copy).then_inc(g_act, 1)
                    act.wait_ge(g_act, g * 8 + (NB + u + 1))
                    for o in range(2):
                        r = slice(o * HD, (o + 1) * HD)
                        act.activation(q_st[r, 2 * u + o, :], y_buf[r, u, :], ACT.Copy).then_inc(q_hi, 1)

                def squares(u):
                    act.wait_ge(ssq_done, g * 2 + (u + 1))
                    act.activation(b_buf[:, u, :], bank[TB[u]][:, :], ACT.Square).then_inc(q_sq, 1)

                def conv_c(u):
                    unit(2 + u)
                    act.activation(a_buf[:, u, :], bank[u][:, :], ACT.Copy).then_inc(g_act, 1)

                def exps(b):
                    w = BAND if 0 < b < NB - 1 else 2 * P
                    act.wait_ge(shift_ready, g * NB + (b + 1))
                    for h in range(HG):
                        act.activation(prob[:, b % 2, h, 0:w], prob[:, b % 2, h, 0:w], ACT.Exp,
                                       bias=sm[:, 1, b, h:h + 1], accum_out=sm[:, 3, b, h:h + 1]).then_inc(exp_done, 1)
                    act.activation(sm[:, 4, b, :], sm[:, 2, b, :], ACT.Exp).then_inc(exp_done, 1)

                def turned_high(ts):
                    for t in ts:
                        act.wait_ge(t_done, g * NT + (t + 1))
                        act.activation(pt_hi[:, t % 2, :], bank[TB[t % 2]][:, :], ACT.Copy).then_inc(pt_h, 1)

                def heads_out(b):
                    act.wait_ge(pv_done, g * NB + (b + 1))
                    for o in range(2):
                        r = slice(o * HD, (o + 1) * HD)
                        act.activation(y_buf[r, :, b * P:(b + 1) * P],
                                       bank[OB][r, :].rearrange("p (u o q) -> p u o q", u=2, o=2)[:, :, o, :],
                                       ACT.Copy, scale=0.5).then_inc(o_free, 1)

                def gate(n):
                    unit(n)
                    if n >= 10:
                        act.wait_ge(ma_done, g * 2 + (n - 9))
                    act.activation(b_buf[:, n % 2, :], bank[n % 2][:, :], ACT.Tanh, scale=0.5).then_inc(g_act, 1)

                high(g, NM, P_MIX + 1)
                query(0)
                squares(0)
                query(1)
                high(g, NM, P_MIX + 2)
                squares(1)
                conv_c(0)
                root(g, 1, 2, NB * HG, 1, 2)
                conv_c(1)
                high(g, NM, P_MIX + 3)
                exps(0)
                turned_high(TS[0])
                exps(1)
                high(g, NM, P_MIX + 4)
                heads_out(0)
                turned_high(TS[1][:2])
                exps(2)
                turned_high(TS[1][2:])
                high(g, NM, P_MIX + 5)
                heads_out(1)
                gate(8)
                turned_high(TS[2][:2])
                exps(3)
                turned_high(TS[2][2:])
                gate(9)
                high(g, NM, P_MIX + 6)
                heads_out(2)
                turned_high(TS[3])
                gate(10)
                heads_out(3)
                gate(11)

            act.wait_ge(units_done, 2 * P_WO)
            for k in range(KT):
                act.wait_ge(mix_free, k + 3)
                act.activation(h_hi[:, k, :], merged[:, k, :], ACT.Copy).then_inc(m_hi, 1)
            for n in range(D // PC):
                high(None, 0, P_WO + n + 1)
                for f in (2 * n, 2 * n + 1):
                    if f in (4, 5):
                        act.wait_ge(b_free, f - 3)
                    else:
                        act.wait_ge(x2_done, f + 1 if f < 4 else f - 1)
                    if f >= 2:
                        act.wait_ge(sum_done, max(f - 2, 1))
                    act.activation(b_buf[:, f % 2, :], xT[:, f, :],
                                   ACT.Square).then_inc(a_free if f in (2, 3) else x2_sq, 1)
            high(None, 0, P_UP + 1)
            root(None, 0, 2 + KV, NB, 1, 2)
            for f in range(KT):
                act.wait_ge(t2_done, f + 1)
                act.activation(h_hi[:, f, :], a_buf[:, f % 2, :], ACT.Identity,
                               bias=mod[:, 3 * KT + f:3 * KT + f + 1]).then_inc(h2_h, 1)

            with act.Fori(0, FF // PC) as j:
                U = 2 * P_UP
                for u in range(2):
                    act.wait_ge(units_done, j * 4 + (U + u + 1))
                    act.activation(pad[u][:, 1:S + 1], bank[2 + u][:, :], ACT.Copy).then_inc(a_free, 1)
                high(j, 2, P_UP + 2)
                for u in range(2):
                    act.wait_ge(conv_done, j * 2 + (u + 1))
                    act.activation(b_buf[:, u, :], a_buf[:, u, :], ACT.Square).then_inc(f_sq, 1)
                for u in range(2):
                    act.wait_ge(z_done, j * 2 + (u + 1))
                    act.activation(b_buf[:, u, :], b_buf[:, u, :], ACT.Tanh,
                                   scale=GELU_C * GELU_S).then_inc(f_th, 1)
                high(j, 2, P_UP + 3)

            def store(q):
                stage = stages[q % 2]
                if q >= 2:
                    act.wait_ge(out_dma[q % 2], 16)
                for u in range(2):
                    act.wait_ge(yt_done, 2 * q + u + 1)
                    act.activation(stage[:, :, u * P:(u + 1) * P],
                                   bank[4 + 2 * (q % 2) + u][:, :].rearrange("p (b n) -> p b n", b=NB),
                                   ACT.Copy).then_inc(a_free, 1)
                act.wait_ge(a_free, 2 + 2 * FF // PC + 2 * q + 2)
                act.dma_start(out_v[:, :, q * PC:(q + 1) * PC], stage).then_inc(out_dma[q % 2], 16)

            stages = [b_buf[:, :, :].rearrange("p u s -> p (u s)").rearrange("p (b n) -> p b n", b=NB),
                      pad_f[:, 0:2 * S].rearrange("p (b n) -> p b n", b=NB)]
            for n in range(P_DOWN, P_END):
                if n + 2 < P_END:
                    high(None, 0, n + 2)
                if n == P_DOWN + 4:
                    store(0)
                if n == P_DOWN + 6:
                    store(1)
                if n == P_DOWN + 10:
                    store(2)
            store(3)
            for s in range(2):
                act.wait_ge(out_dma[s], 32)

        @block.tensor
        def _(pe):
            def three(dst, w_h, w_l, rhs_hi, rhs_lo, first, last):
                pe.matmul(dst, w_h, rhs_hi, start=first, stop=False)
                pe.matmul(dst, w_h, rhs_lo, start=False, stop=False)
                return pe.matmul(dst, w_l, rhs_hi, start=False, stop=last)

            pe.wait_ge(const_done, 1)
            pe.wait_ge(c_in, 16)
            pe.transpose(bank[5][:, 0:KT], par_rows[0:KT, 0:P], ident[0:KT, 0:KT]).then_inc(c_t, 1)
            for b in range(NB):
                pe.wait_ge(x_in[b], 16)
            for m in range(KT):
                if m >= 4:
                    pe.wait_ge(xt_out, m - 3)
                for b in range(NB):
                    mm = pe.transpose(bank[m % 4][:, b * P:(b + 1) * P], x_nat[:, b, m * P:(m + 1) * P], ident[:, :])
                mm.then_inc(xt_done, 1)
                if m == 3:
                    pe.wait_ge(const_done, 2)
                    pe.wait_ge(xd_done, NB)
                    pe.matmul(bank[4][:, :], ones[:, :], y_buf[:, 1, :], start=True, stop=True).then_inc(xr_done, 1)
            pe.wait_ge(par_in, 16 * 10)
            for t, n in enumerate((ROWS1, ROWS2)):
                pe.transpose(bank[6 + t][:, 0:n], par_rows[0:n, t * P:(t + 1) * P], ident[0:n, 0:n]).then_inc(par_t, 1)

            def mod_turn(a):
                pe.wait_ge(gemv_done, (a + 1) * KT)
                for s in range(2):
                    for f in range(HT):
                        mm = pe.transpose(bank[6 + s][:, f * P:(f + 1) * P], acc0[:, a, s, f * P:(f + 1) * P],
                                          ident[:, :])
                    mm.then_inc(mod_done, 1)

            def token_major(n, ks):
                for k in ks:
                    pe.wait_ge(h_ready, k + 1)
                    for b in range(NB):
                        dst = bank[4 * n + b][:, 0:PC].rearrange("p (u n) -> p u n", u=2)
                        t = slice(b * P, (b + 1) * P)
                        mm = three(dst, h_hi[:, k, t], h_lo[:, k, t], w_hi[:, n, :, k, :], w_lo[:, n, :, k, :],
                                   k == 0, k == KT - 1)
                        if k == KT - 1 and b >= 2:
                            mm.then_inc(units_done, 1)

            pe.wait_ge(par_c, 2)
            mod_turn(0)
            pe.wait_ge(lo_ready, 2)
            token_major(0, range(HT))
            mod_turn(1)
            token_major(0, range(HT, KT))
            pe.wait_ge(lo_ready, 4)
            token_major(1, range(KT))
            pe.wait_ge(kn_ready, 1)
            for f in range(2):
                for b in range(NB):
                    mm = pe.transpose(bank[SC[f]][:, b * P:(b + 1) * P],
                                      k_nat[:, b * PC + f * P:b * PC + (f + 1) * P], ident[:, :])
                mm.then_inc(kt_done, 1)

            with pe.Fori(0, KV) as g:
                def unit_waits(n):
                    pe.wait_ge(lo_ready, g * (2 * NM) + (2 * P_MIX + n + 1))
                    if n in (6, 7, 8, 9):
                        pe.wait_ge(g_dve, g * 4 + (n - 5))
                    else:
                        pe.wait_ge(g_act, g * 8 + {0: 3, 1: 4, 2: 5, 3: 6, 4: 7, 5: 8, 10: 9, 11: 10}[n])

                def unit_half(n, a):
                    s, u = (n // 2) % 2, n % 2
                    for k in range(4 * a, 4 * a + 4):
                        mm = three(bank[u][:, :], w_hi[:, s, u, k, :], w_lo[:, s, u, k, :],
                                   h_hi[:, k, :], h_lo[:, k, :], k == 0, k == KT - 1)
                    if a:
                        mm.then_inc(units_done, 1)

                def query_turn(u):
                    pe.wait_ge(g_act, g * 8 + (NB + u + 1))
                    pe.wait_ge(t_free, g * NT + 2)
                    for b in range(NB):
                        mm = pe.transpose(bank[TB[u]][:, b * P:(b + 1) * P], y_buf[:, u, b * P:(b + 1) * P],
                                          ident[:, :])
                    mm.then_inc(ssq_done, 1)

                def scores(b, hs):
                    j0, j1 = max(b - 1, 0) * P, min(b + 2, NB) * P
                    for h in hs:
                        pe.wait_ge(q_lo, g * HG + (h + 1))
                        pe.wait_ge(score_free, g * (NB * HG) + (b * HG + h + 1))
                        dst = bank[SC[h % 2]][:, 0:j1 - j0]
                        for p in range(2):
                            mm = pe.matmul(dst, q_st[:, h, b * P:(b + 1) * P],
                                           k_st[:, p, bass.ds(g, 1), j0:j1].rearrange("p a n -> p (a n)"),
                                           start=(p == 0), stop=(p == 1))
                        mm.then_inc(s_done, 1)

                def turn(b, i):
                    t = TS[b][i]
                    pe.wait_ge(p_ready, g * (NB * HG) + (b * HG + HG))
                    pe.wait_ge(t_free, g * NT + (t + 1))
                    for h in range(HG):
                        mm = pe.transpose(bank[TB[t % 2]][:, h * P:(h + 1) * P],
                                          prob[:, b % 2, h, i * P:(i + 1) * P], ident[:, :])
                    mm.then_inc(t_done, 1)

                def values(b, i):
                    t = TS[b][i]
                    pe.wait_ge(t_free, g * NT + (t + 3))
                    if i == 0:
                        pe.wait_ge(v_staged, g * 2 + 2)
                        pe.wait_ge(o_free, g * (2 * NB) + (2 * b + 1))
                    kb = max(b - 1, 0) + i
                    last = i == len(TS[b]) - 1
                    mm = three(bank[OB][:, :], v_hi[:, kb], v_lo[:, kb], pt_hi[:, t % 2, :], pt_lo[:, t % 2, :],
                               i == 0, last)
                    if last:
                        mm.then_inc(pv_done, 1)

                def ada_turn(a):
                    pe.wait_ge(gemv_done, g * KT + 3 * KT)
                    pe.wait_ge(m_free, g * 2 + (a + 1))
                    for f in range(HT):
                        mm = pe.transpose(bank[MB][:, f * P:(f + 1) * P],
                                          acc[:, (a * HT + f) * P:(a * HT + f + 1) * P], ident[:, :])
                    mm.then_inc(mod_done, 1)

                for slot in range(4 * NM):
                    if slot in (3, 5):
                        query_turn((slot - 3) // 2)
                    for b in range(NB):
                        r = slot - 3 * b
                        if r == 12:
                            turn(b, 0)
                            turn(b, 1)
                        if r == 13:
                            values(b, 0)
                            if len(TS[b]) == 3:
                                turn(b, 2)
                            values(b, 1)
                        if r == 14 and len(TS[b]) == 3:
                            values(b, 2)
                    for b in range(NB):
                        if slot - 3 * b == 7:
                            scores(b, (0, 1))
                        if slot - 3 * b == 8:
                            scores(b, (2, 3))
                    if slot in (14, 17):
                        ada_turn((slot - 14) // 3)
                    if slot % 2 == 0:
                        unit_waits(slot // 2)
                    unit_half(slot // 2, slot % 2)

            def tile_k(n, u, k, dst, rhs, k_off, first, last):
                return three(bank[dst][:, :], w_hi[:, n % 2, u, k, :], w_lo[:, n % 2, u, k, :],
                             rhs[0][:, k_off + k, :], rhs[1][:, k_off + k, :], first, last)

            def arriving(i, per, n, banks, rhs, arrival):
                pe.wait_ge(lo_ready, at(i, 2 * per, 2 * n + 2))
                for k in range(KT):
                    pe.wait_ge(*arrival(k))
                    for u in range(2):
                        mm = tile_k(n, u, k, banks[u], rhs, 0, k == 0, k == KT - 1)
                        if k == KT - 1:
                            mm.then_inc(units_done, 1)

            def pair(i, per, n, banks, rhs, kn=8, k_off=0, first=True, last=True):
                for u in range(2):
                    pe.wait_ge(lo_ready, at(i, 2 * per, 2 * n + u + 1))
                    for k in range(kn):
                        mm = tile_k(n, u, k, banks[u], rhs, k_off, first and k == 0, last and k == kn - 1)
                    mm.then_inc(units_done, 1)

            arriving(None, 0, P_WO, (0, 1), (h_hi, h_lo),
                     lambda k: (m_lo, k + 1) if k < KT - 2 else (m_lo_dve, k + 3 - KT))
            pe.wait_ge(m_free, 2 * KV + 1)
            for n in range(1, D // PC):
                pair(None, 0, P_WO + n, (2 * n, 2 * n + 1), (h_hi, h_lo))
            pe.wait_ge(sum_done, KT - 1)
            for b in range(NB):
                mm = pe.transpose(bank[0][:, b * P:(b + 1) * P], y_buf[:, 0, b * P:(b + 1) * P], ident[:, :])
            mm.then_inc(ss_done, 1)
            pe.wait_ge(diag_done, NB)
            pe.matmul(bank[1][:, :], ones[:, :], y_buf[:, 1, :], start=True, stop=True).then_inc(r_done, 1)

            with pe.Fori(0, FF // PC) as j:
                pe.wait_ge(a_free, j * 2 + 2)
                arriving(j, 2, P_UP, (2, 3), (h_hi, h_lo), lambda k: (h2_ready, k + 1))
                pe.wait_ge(b_free, j * 2 + 2)
                pair(j, 2, P_UP + 1, (4, 5), (h_hi, h_lo))

            with pe.Fori(0, 2) as i:
                def turn_out(q):
                    for u in range(2):
                        pe.wait_ge(ffn_tiles, i * 4 + (FT + 2 * q + u + 1))
                        pe.wait_ge(a_free, i * 4 + (2 + FT - 2 + 2 * q))
                        for b in range(NB):
                            mm = pe.transpose(bank[4 + 2 * q + u][:, b * P:(b + 1) * P],
                                              (a_buf, y_buf)[q][:, u, b * P:(b + 1) * P], ident[:, :])
                        mm.then_inc(yt_done, 1)

                for q in range(2):
                    for cc in range(3):
                        if cc == 0:
                            pe.wait_ge(ffn_tiles, i * 4 + (FT - 2 + 2 * q))
                        if cc == 2:
                            pe.wait_ge(ffn_tiles, FT)
                        pair(i, 6, P_DOWN + 3 * q + cc, (2 * q, 2 * q + 1), (g_hi, g_lo), kn=CH[cc], k_off=8 * cc,
                             first=cc == 0, last=cc == 2)
                        if q == 1 and cc == 0:
                            turn_out(0)
                turn_out(1)

        @block.vector
        def _(dve):
            steps = Tally(dve, dve_done)

            def rsqrt(i, per, n, cols, ss, scale, dst, fold=1.0):
                v, s, r, t = (st[:, m, 0:cols] for m in (1, 2, 3, 4))
                dve.tensor_scalar(v, ss, scale, EPS, MUL, ADD).then_inc(var_ready, 1)
                dve.wait_ge(root_ready, at(i, per, n + 1))
                steps.link(dve.reciprocal(r, s))
                steps.link(dve.tensor_tensor(t, r, r, MUL))
                steps.link(dve.tensor_tensor(t, t, v, MUL))
                steps.link(dve.tensor_scalar(t, t, -0.5 * fold, 1.5 * fold, MUL, ADD))
                steps.link(dve.tensor_tensor(dst, r, t, MUL))

            for u in range(2):
                dve.memset(pad_f[:, u * (S + 2):(u + 1) * (S + 2)], 0.0).then_inc(mix_free, 1)
            dve.wait_ge(const_done, 3)
            steps.link(dve.tensor_scalar(a_buf[:, 0, 0:BAND], ndist[:, :], -1.0, None, MUL))
            dve.tensor_tensor(ndist[:, :], ndist[:, :], a_buf[:, 0, 0:BAND], ALU.min).then_inc(dist_done, 1)
            dve.wait_ge(c_th, 1)
            steps.link(dve.scalar_tensor_tensor(c_act[:, 0, :], c_act[:, 1, :], 1.0, bank[5][:, 0:KT], ADD, MUL))
            steps.link(dve.tensor_scalar(c_act[:, 0, :], c_act[:, 0, :], 0.5, None, MUL))
            dve.wait_ge(x_sq, NB)
            rsqrt(None, 0, 0, NB, st[:, 0, 0:NB], 1.0 / D, st[:, 5, 0:NB])
            for b in range(NB):
                dve.tensor_scalar(y_buf[:, 1, b * P:(b + 1) * P], ident[:, :], st[:, 5, b:b + 1], None,
                                  MUL).then_inc(xd_done, 1)

            def gemv0(n):
                a, k = n // KT, n % KT
                dve.wait_ge(ada0_in[n % RING], 16 * (n // RING) + 16)
                if k == 0:
                    ins = dve.tensor_scalar(acc0[:, a], ada0[:, n % RING], c_act[:, 0, 0:1], None, MUL)
                else:
                    dve.wait_ge(gemv_done, n)
                    ins = dve.scalar_tensor_tensor(acc0[:, a], ada0[:, n % RING], c_act[:, 0, k:k + 1], acc0[:, a],
                                                   MUL, ADD)
                ins.then_inc(gemv_done, 1)

            def normed(k):
                dve.wait_ge(xt_out, k + 1)
                dve.wait_ge(xr_done, 1)
                steps.inc(dve.tensor_tensor(hT[:, k, :], xT[:, k, :], bank[4][:, :], MUL))

            def mods(a):
                for s in range(2):
                    dve.wait_ge(mod_done, 2 * a + s + 1)
                    steps.inc(dve.tensor_reduce(mod[:, s * KT + a * HT:s * KT + (a + 1) * HT],
                                                bank[6 + s][:, :].rearrange("p (f n) -> p f n", n=P), AX.X, ADD))
                dve.wait_ge(dve_done, steps.n)
                m2, b2 = (t.rearrange("p (s k) -> p s k", s=2)[:, :, a * HT:(a + 1) * HT]
                          for t in (mod[:, 0:2 * KT], par[:, PA_B:PA_B + 2 * KT]))
                dve.wait_ge(par_c, 2)
                steps.link(dve.tensor_tensor(m2, m2, b2, ADD))
                steps.link(dve.scalar_tensor_tensor(amp[:, 0, a * HT:(a + 1) * HT],
                                                    mod[:, KT + a * HT:KT + (a + 1) * HT], 1.0,
                                                    par[:, PA_G1 + a * HT:PA_G1 + (a + 1) * HT], ADD, MUL))

            def h_low(k):
                dve.wait_ge(h_h, k + 1)
                dve.tensor_tensor(h_lo[:, k, :], hT[:, k, :], h_hi[:, k, :], SUB).then_inc(h_ready, 1)

            def modulate(a):
                for k in range(a * HT, (a + 1) * HT):
                    dve.tensor_scalar(hT[:, k, :], hT[:, k, :], amp[:, 0, k:k + 1], mod[:, k:k + 1],
                                      MUL, ADD).then_inc(h_f, 1)
                    if k > a * HT:
                        h_low(k - 1)
                h_low((a + 1) * HT - 1)

            for n in range(KT):
                gemv0(n)
                if n >= HT:
                    normed(n - HT)
            mods(0)
            modulate(0)
            for n in range(KT, 2 * KT):
                gemv0(n)
                if n < KT + HT:
                    normed(n - HT)
            mods(1)
            modulate(1)

            dve.wait_ge(g_act, NB)
            steps.link(dve.tensor_tensor(k_sq, k_nat, k_nat, MUL))
            steps.link(dve.tensor_reduce(st[:, 0, :], k_sq.rearrange("p (a d) -> p a d", d=HD), AX.X, ADD))
            rsqrt(None, 0, 1, NB * KV, st[:, 0, 0:NB * KV], 1.0 / HD, st[:, 6, :])
            dve.tensor_tensor(k_nat.rearrange("p (a d) -> p a d", d=HD), k_nat.rearrange("p (a d) -> p a d", d=HD),
                              st[:, 6, :].unsqueeze(2).to_broadcast([P, NB * KV, HD]), MUL).then_inc(kn_ready, 1)
            dve.wait_ge(units_done, 4)
            for b, done in ((0, t_free), (1, t_free), (3, m_free)):
                dve.tensor_copy(v_nat[:, b, :], bank[4 + b][:, 0:PC]).then_inc(done, 1)
            for f in range(2):
                dve.wait_ge(kt_done, f + 1)
                dve.tensor_scalar(k_T[:, f, :], bank[SC[f]][:, :], par[:, PA_KG:PA_KG + 1], par[:, PA_QG:PA_QG + 1],
                                  MUL, MUL).then_inc(score_free, 1)
            dve.wait_ge(score_free, 2)
            for j in range(KV):
                a = (j % 2) * HD
                dve.wait_ge(kh_done, 2 * j + 2)
                for o in range(2):
                    dve.tensor_tensor(k_st[o * HD:(o + 1) * HD, 1, j, :], k_T[a:a + HD, j // 2, :],
                                      k_st[a:a + HD, 0, j, :], SUB).then_inc(kl_done, 1)
            dve.wait_ge(o_free, 1)
            dve.wait_ge(m_free, 1)
            dve.wait_ge(t_free, 2)
            dve.wait_ge(kl_done, 2 * KV)
            dve.wait_ge(sink_in, 16)

            with dve.Fori(0, KV) as g:
                steps.enter(g, STEPS)

                def gemv(k):
                    dve.wait_ge(ada_in[k % 2], g * (8 * KT) + (16 * (k // 2) + 16))
                    if k == 0:
                        ins = dve.tensor_scalar(acc[:, :], ada[:, 0, :], c_act[:, 0, 0:1], None, MUL)
                    else:
                        dve.wait_ge(gemv_done, g * KT + (2 * KT + k))
                        ins = dve.scalar_tensor_tensor(acc[:, :], ada[:, k % 2, :], c_act[:, 0, k:k + 1], acc[:, :],
                                                       MUL, ADD)
                    ins.then_inc(gemv_done, 1)

                def stage_values():
                    v = v_nat[:, :, bass.ds(g * HD, HD)]
                    for o in range(2):
                        steps.inc(dve.tensor_scalar(v_hi[:, :, o, :], v, 1.0, None, MUL))
                    dve.wait_ge(dve_done, steps.turn + steps.n)
                    for o in range(2):
                        dve.tensor_tensor(v_lo[:, :, o, :], v, v_hi[:, :, o, :], SUB).then_inc(v_staged, 1)

                def query_low(u):
                    dve.wait_ge(q_hi, g * HG + (2 * u + 2))
                    for o in range(2):
                        r, w = slice(o * HD, (o + 1) * HD), slice((1 - o) * HD, (2 - o) * HD)
                        dve.tensor_tensor(q_st[w, 2 * u + o, :], y_buf[r, u, :], q_st[r, 2 * u + o, :],
                                          SUB).then_inc(q_lo, 1)

                def query_sums(u):
                    dve.wait_ge(q_sq, g * 2 + (u + 1))
                    steps.link(dve.tensor_reduce(st[:, 0, :].rearrange("p (b h) -> p b h", b=NB)[:, :, 2 * u:2 * u + 2],
                                                 b_buf[:, u, :].rearrange("p (b h d) -> p b h d", b=NB, h=2),
                                                 AX.X, ADD))

                def query_norm():
                    rsqrt(g, 1, 2, NB * HG, st[:, 0, :], 1.0 / HD, sm[:, 6, :, :].rearrange("p b h -> p (b h)"), RS)

                def ada_sums(a):
                    dve.wait_ge(mod_done, g * 2 + (4 + a + 1))
                    dve.tensor_reduce(st[:, 7, a * HT:(a + 1) * HT],
                                      bank[MB][:, :].rearrange("p (f n) -> p f n", n=P), AX.X, ADD).then_inc(m_free, 1)

                def take(b, hs):
                    w = P * len(TS[b])
                    c0 = P if b == 0 else 0
                    for h in hs:
                        dve.wait_ge(s_done, g * (NB * HG) + (b * HG + h + 1))
                        if b == 0 and h == 0:
                            dve.wait_ge(bias_done, g + HG)
                        dve.scalar_tensor_tensor(prob[:, b % 2, h, 0:w], bank[SC[h % 2]][:, 0:w], sm[:, 6, b, h:h + 1],
                                                 bias[:, h, c0:c0 + w], MUL, ADD).then_inc(score_free, 1)

                def shift(b):
                    w = P * len(TS[b])
                    dve.wait_ge(score_free, g * (NB * HG) + (b * HG + HG + 2))
                    steps.link(dve.tensor_reduce(sm[:, 0, b, :], prob[:, b % 2, :, 0:w], AX.X, MAX))
                    steps.link(dve.tensor_tensor(sm[:, 0, b, :], sm[:, 0, b, :], sink_b[:, bass.ds(g * HG, HG)], MAX))
                    steps.link(dve.tensor_scalar(sm[:, 1, b, :], sm[:, 0, b, :], -1.0, None, MUL))
                    dve.tensor_tensor(sm[:, 2, b, :], sm[:, 1, b, :], sink_b[:, bass.ds(g * HG, HG)],
                                      ADD).then_inc(shift_ready, 1)

                def normalise(b):
                    w = P * len(TS[b])
                    dve.wait_ge(exp_done, g * (NB * (HG + 1)) + (b + 1) * (HG + 1))
                    steps.link(dve.tensor_tensor(sm[:, 5, b, :], sm[:, 3, b, :], sm[:, 4, b, :], ADD))
                    steps.link(dve.reciprocal(sm[:, 5, b, :], sm[:, 5, b, :]))
                    for h in range(HG):
                        dve.tensor_scalar(prob[:, b % 2, h, 0:w], prob[:, b % 2, h, 0:w], sm[:, 5, b, h:h + 1], None,
                                          MUL).then_inc(p_ready, 1)

                def turned_low(ts):
                    for t in ts:
                        dve.wait_ge(pt_h, g * NT + (t + 1))
                        dve.tensor_tensor(pt_lo[:, t % 2, :], bank[TB[t % 2]][:, :], pt_hi[:, t % 2, :],
                                          SUB).then_inc(t_free, 1)

                def conv_in(u):
                    dve.wait_ge(units_done, g * (2 * NM) + (2 * P_MIX + 4 + u + 1))
                    dve.wait_ge(g_act, g * 8 + (NB + 3 + u))
                    dve.tensor_tensor(pad[u][:, 1:S + 1], bank[u][:, :], a_buf[:, u, :], MUL).then_inc(g_dve, 1)

                def taps(u):
                    def w(tap):
                        return par[:, bass.ds(g * 2 + (PA_CW + tap * KT + u), 1)]
                    dve.wait_ge(g_dve, g * 4 + (u + 1))
                    steps.link(dve.tensor_scalar(a_buf[:, u, :], pad[u][:, 0:S], w(0), None, MUL))
                    for tap in (1, 2):
                        steps.link(dve.scalar_tensor_tensor(a_buf[:, u, :], pad[u][:, tap:tap + S], w(tap),
                                                            a_buf[:, u, :], MUL, ADD))

                def conv_out(u):
                    dve.wait_ge(units_done, g * (2 * NM) + (2 * P_MIX + 6 + u + 1))
                    dve.scalar_tensor_tensor(a_buf[:, u, :], bank[u][:, :], 0.5, a_buf[:, u, :],
                                             MUL, MUL).then_inc(g_dve, 1)

                def gate_a(u):
                    dve.wait_ge(g_dve, g * 4 + (u + 3))
                    dve.wait_ge(g_act, g * 8 + (NB + 5 + u))
                    dve.scalar_tensor_tensor(a_buf[:, u, :], b_buf[:, u, :], 1.0, a_buf[:, u, :],
                                             ADD, MUL).then_inc(ma_done, 1)

                def merge(u):
                    dve.wait_ge(g_act, g * 8 + (NB + 7 + u))
                    dve.wait_ge(ma_done, g * 2 + (u + 1))
                    steps.link(dve.scalar_tensor_tensor(b_buf[:, u, :], b_buf[:, u, :], 1.0, y_buf[:, u, :], ADD, MUL))
                    dve.tensor_tensor(merged[:, bass.ds(g * 2 + u, 1), :].rearrange("p a n -> p (a n)"),
                                      b_buf[:, u, :], a_buf[:, u, :], ADD).then_inc(mix_free, 1)

                gemv(0)
                gemv(1)
                stage_values()
                query_low(0)
                gemv(2)
                gemv(3)
                query_sums(0)
                query_low(1)
                gemv(4)
                query_sums(1)
                query_norm()
                gemv(5)
                take(0, (0, 1))
                gemv(6)
                take(0, (2, 3))
                shift(0)
                gemv(7)
                conv_in(0)
                take(1, (0, 1))
                normalise(0)
                take(1, (2, 3))
                shift(1)
                turned_low(TS[0])
                conv_in(1)
                taps(0)
                take(2, (0, 1))
                normalise(1)
                taps(1)
                take(2, (2, 3))
                shift(2)
                conv_out(0)
                turned_low(TS[1])
                ada_sums(0)
                conv_out(1)
                take(3, (0, 1))
                normalise(2)
                take(3, (2, 3))
                shift(3)
                turned_low(TS[2][:2])
                gate_a(0)
                turned_low(TS[2][2:])
                ada_sums(1)
                normalise(3)
                gate_a(1)
                turned_low(TS[3])
                dve.wait_ge(m_free, g * 2 + 3)
                steps.link(dve.tensor_tensor(mod[:, bass.ds(g * KT + 2 * KT, KT)], st[:, 7, 0:KT],
                                             par[:, bass.ds(g * KT + (PA_B + 2 * KT), KT)], ADD))
                dve.wait_ge(o_free, g * (2 * NB) + (2 * NB + 1))
                merge(0)
                merge(1)
                steps.leave(KV)

            steps.link(dve.scalar_tensor_tensor(amp[:, 1, :], mod[:, 4 * KT:5 * KT], 1.0, par[:, PA_G2:PA_G2 + KT],
                                                ADD, MUL))
            for k in range(KT - 2, KT):
                dve.wait_ge(m_hi, k + 1)
                dve.tensor_tensor(h_lo[:, k, :], merged[:, k, :], h_hi[:, k, :], SUB).then_inc(m_lo_dve, 1)
            for f in range(KT):
                dve.wait_ge(units_done, 2 * P_WO + f + 1)
                dve.scalar_tensor_tensor(xT[:, f, :], bank[f][:, :], mod[:, 2 * KT + f:2 * KT + f + 1], xT[:, f, :],
                                         MUL, ADD).then_inc(b_free if f in (4, 5) else x2_done, 1)
                if f >= 1:
                    g_ = f - 1
                    if g_ in (2, 3):
                        dve.wait_ge(a_free, g_ - 1)
                    else:
                        dve.wait_ge(x2_sq, g_ + 1 if g_ < 2 else g_ - 1)
                    square_add(dve, g_, sum_done, y_buf, b_buf, ADD)
            dve.wait_ge(x2_sq, KT - 2)
            square_add(dve, KT - 1, sum_done, y_buf, b_buf, ADD)
            dve.wait_ge(ss_done, 1)
            steps.link(dve.tensor_reduce(st[:, 0, 0:NB], bank[0][:, :].rearrange("p (b n) -> p b n", n=P), AX.X, ADD))
            rsqrt(None, 0, 2 + KV, NB, st[:, 0, 0:NB], 1.0 / D, st[:, 5, 0:NB])
            for b in range(NB):
                dve.tensor_scalar(y_buf[:, 1, b * P:(b + 1) * P], ident[:, :], st[:, 5, b:b + 1], None,
                                  MUL).then_inc(diag_done, 1)
            dve.wait_ge(r_done, 1)

            def h2_low(f):
                dve.wait_ge(h2_h, f + 1)
                dve.scalar_tensor_tensor(h_lo[:, f, :], a_buf[:, f % 2, :], mod[:, 3 * KT + f:3 * KT + f + 1],
                                         h_hi[:, f, :], ADD, SUB).then_inc(h2_ready, 1)

            for f in range(KT):
                if f >= 2:
                    dve.wait_ge(h2_ready, f - 1)
                dve.scalar_tensor_tensor(a_buf[:, f % 2, :], xT[:, f, :], amp[:, 1, f:f + 1], bank[1][:, :],
                                         MUL, MUL).then_inc(t2_done, 1)
                if f >= 1:
                    h2_low(f - 1)
            h2_low(KT - 1)

            with dve.Fori(0, FF // PC) as j:
                steps.enter(j, STEPS_UP)
                for u in range(2):
                    def w(row):
                        return par[:, bass.ds(j * 2 + (row + u), 1)]
                    dve.wait_ge(a_free, j * 2 + (2 + u + 1))
                    steps.link(dve.tensor_scalar(a_buf[:, u, :], pad[u][:, 0:S], w(PA_FW), w(PA_FB), MUL, ADD))
                    steps.link(dve.scalar_tensor_tensor(a_buf[:, u, :], pad[u][:, 1:S + 1], w(PA_FW + FT),
                                                        a_buf[:, u, :], MUL, ADD))
                    dve.scalar_tensor_tensor(a_buf[:, u, :], pad[u][:, 2:S + 2], w(PA_FW + 2 * FT), a_buf[:, u, :],
                                             MUL, ADD).then_inc(conv_done, 1)
                for u in range(2):
                    dve.wait_ge(f_sq, j * 2 + (u + 1))
                    dve.scalar_tensor_tensor(b_buf[:, u, :], b_buf[:, u, :], 1.0 / GELU_C, a_buf[:, u, :],
                                             ADD, MUL).then_inc(z_done, 1)
                for u in range(2):
                    dve.wait_ge(f_th, j * 2 + (u + 1))
                    steps.link(dve.scalar_tensor_tensor(y_buf[:, u, :], b_buf[:, u, :], 1.0, a_buf[:, u, :], ADD, MUL))
                for u in range(2):
                    dve.wait_ge(units_done, j * 4 + (2 * P_UP + 2 + u + 1))
                    dve.scalar_tensor_tensor(y_buf[:, u, :], bank[4 + u][:, :], 0.5, y_buf[:, u, :],
                                             MUL, MUL).then_inc(b_free, 1)
                for u in range(2):
                    hi = g_hi[:, bass.ds(j * 2 + u, 1), :].rearrange("p a n -> p (a n)")
                    lo = g_lo[:, bass.ds(j * 2 + u, 1), :].rearrange("p a n -> p (a n)")
                    dve.wait_ge(b_free, j * 2 + (2 + u + 1))
                    steps.link(dve.tensor_scalar(hi, y_buf[:, u, :], 1.0, None, MUL))
                    dve.tensor_tensor(lo, y_buf[:, u, :], hi, SUB).then_inc(ffn_tiles, 1)
                steps.leave(FF // PC)

            with dve.Fori(0, 2) as i:
                for q in range(2):
                    for u in range(2):
                        f = 2 * q + u
                        dve.wait_ge(units_done, i * 12 + (2 * P_DOWN + 6 * q + 4 + u + 1))
                        dve.scalar_tensor_tensor((a_buf, y_buf)[q][:, u, :], bank[2 * q + u][:, :],
                                                 mod[:, bass.ds(i * 4 + (5 * KT + f), 1)],
                                                 xT[:, bass.ds(i * 4 + f, 1), :].rearrange("p a n -> p (a n)"),
                                                 MUL, ADD).then_inc(ffn_tiles, 1)


def square_add(dve, f, sum_done, y_buf, b_buf, ADD):
    if f == 0:
        return
    if f == 1:
        ins = dve.tensor_tensor(y_buf[:, 0, :], b_buf[:, 0, :], b_buf[:, 1, :], ADD)
    else:
        dve.wait_ge(sum_done, f - 1)
        ins = dve.tensor_tensor(y_buf[:, 0, :], y_buf[:, 0, :], b_buf[:, f % 2, :], ADD)
    ins.then_inc(sum_done, 1)


_INS = ["x", "c", "w_ada", "b_ada", "norm1_gain", "w_in", "conv_w", "q_gain", "k_gain", "sink", "w_o",
        "norm2_gain", "w_up", "ffn_conv_w", "ffn_conv_b", "w_down"]


def kernel(**inputs):
    import numpy as _np
    import concourse.bacc as _bacc
    from concourse import mybir as _mybir
    from concourse.bass_utils import run_bass_kernel_spmd as _run

    nc = _bacc.Bacc("TRN2", target_bir_lowering=False, num_devices=1)
    arrays, args = {}, []
    for name in _INS:
        a = _np.ascontiguousarray(inputs[name])
        arrays[f"in_{name}_dram"] = a
        args.append(nc.dram_tensor(f"in_{name}_dram", a.shape, _mybir.dt.from_np(a.dtype), kind="ExternalInput").ap())
    shape = inputs["x"].shape
    out = nc.dram_tensor("out_0_dram", shape, _mybir.dt.float32, kind="ExternalOutput").ap()
    encoder_block(nc, *args, out)
    r = _run(nc, [arrays], core_ids=[0])
    return r.results[0]["out_0_dram"]
```

```python
import concourse.bass as bass
from concourse import mybir
from contextlib import ExitStack
import numpy as np


class Tally:

    def __init__(self, eng, sem):
        self.eng, self.sem, self.n, self.turn = eng, sem, 0, 0

    def enter(self, i, per):
        self.start, self.per, self.turn = self.n, per, i * per

    def leave(self, turns):
        assert self.n - self.start == self.per, (self.n - self.start, self.per)
        self.n, self.turn = self.start + turns * self.per, 0

    def inc(self, ins):
        ins.then_inc(self.sem, 1)
        self.n += 1

    def link(self, ins):
        self.inc(ins)
        self.eng.wait_ge(self.sem, self.turn + self.n)


def encoder_block(nc, x, c, w_ada, b_ada, norm1_gain, w_in, conv_w, q_gain, k_gain, sink, w_o,
                  norm2_gain, w_up, ffn_conv_w, ffn_conv_b, w_down, out):
    fp32, f32r = mybir.dt.float32, mybir.dt.float32r
    ALU, ACT, AX = mybir.AluOpType, mybir.ActivationFunctionType, mybir.AxisListType
    MUL, ADD, SUB, MAX = ALU.mult, ALU.add, ALU.subtract, ALU.max

    P = 128
    S, D = x.shape[1], x.shape[2]
    KT = D // P
    NB = S // P
    HD = q_gain.shape[1]
    H = D // HD
    KV = H // 4
    HG = H // KV
    FF = w_down.shape[1]
    FT = FF // P
    PC = 2 * P
    EPS = 1e-6
    BAND = 3 * P
    MASKED = -1e35
    GELU_C, GELU_S = 0.044715, float(np.sqrt(2 / np.pi))
    RS = 1.0 / np.sqrt(HD)

    COL_B, COL_C, COL_U, COL_Q = 0, D, 2 * D, 3 * D
    COL_K = 4 * D
    COL_V = COL_K + KV * HD
    COL_GA = COL_V + KV * HD
    COL_GB = COL_GA + D
    MIX = [COL_Q, COL_C, COL_U, COL_B, COL_GA, COL_GB]
    NM = len(MIX)

    P_MIX = 2
    P_WO = P_MIX + NM * KV
    P_UP = P_WO + D // PC
    P_DOWN = P_UP + 2 * (FF // PC)
    CH = [8, 8, FT - 16]
    P_END = P_DOWN + len(CH) * (D // PC)

    PA_C, PA_B, PA_G1, PA_G2, PA_CW = 0, KT, 7 * KT, 8 * KT, 9 * KT
    PA_QG, PA_KG = 12 * KT, 12 * KT + 1
    ROWS1 = 12 * KT + 2
    PA_FW, PA_FB = ROWS1, ROWS1 + 3 * FT
    ROWS2 = 4 * FT
    HT = KT // 2
    RING = 8
    PE_ADA = [KT]
    DVE_ADA = [n for n in range(2 * KT) if n not in PE_ADA]
    G0 = len(DVE_ADA)

    def k_rows(w):
        return w[0].rearrange("(k p) n -> p k n", p=P)

    wi, wo, wu, wd = k_rows(w_in), k_rows(w_o), k_rows(w_up), k_rows(w_down)
    out_v = out[0].rearrange("(b p) n -> p b n", p=P)

    ctx = ExitStack()
    with ctx:
        def sb(name, shape, dt=fp32, into=ctx):
            return into.enter_context(nc.sbuf_tensor(name, shape, dt))

        def sem(name):
            return ctx.enter_context(nc.semaphore(name))

        h_hi = sb("h_hi", [P, KT, S], f32r)
        h_lo = sb("h_lo", [P, KT, S], f32r)
        xT = sb("xT", [P, KT, S])
        w_raw = sb("w_raw", [P, 2, 8, PC])
        w_hi = sb("w_hi", [P, 2, 2, 8, P], f32r)
        w_lo = sb("w_lo", [P, 2, 2, 8, P], f32r)
        par = sb("par", [P, ROWS1 + ROWS2])
        mod = sb("mod", [P, 6 * KT])
        amp = sb("amp", [P, 2, KT])
        c_act = sb("c_act", [P, 2, KT])
        ident = sb("ident", [P, P])
        ones = sb("ones", [P, P])
        sink_b = sb("sink_b", [P, H])
        ndist = sb("ndist", [P, BAND])
        st = sb("st", [P, 8, 16])
        sm = sb("sm", [P, 7, NB, HG])
        a_buf = sb("a_buf", [P, 2, S])
        b_buf = sb("b_buf", [P, 2, S])
        y_buf = sb("y_buf", [P, 2, S])
        pad_f = sb("pad_f", [P, 2 * (S + 2)])
        pad = [pad_f[:, u * (S + 2):(u + 1) * (S + 2)] for u in range(2)]

        start = ExitStack()
        x_nat = sb("x_nat", [P, NB, D], into=start)
        hT = sb("hT", [P, KT, S], into=start)
        ada0 = sb("ada0", [P, RING, 2, D // 2], into=start)
        acc0 = sb("acc0", [P, 2, 2, D // 2], into=start)
        c_b = sb("c_b", [P, P], into=start)
        start.close()

        mixer = ExitStack()
        merged = sb("merged", [P, KT, S], into=mixer)
        k_st = sb("k_st", [P, 2, KV, S], f32r, into=mixer)
        v_nat = sb("v_nat", [P, NB, KV * HD], into=mixer)
        q_st = sb("q_st", [P, HG, S], f32r, into=mixer)
        v_st = sb("v_st", [P, NB, 2, HD], f32r, into=mixer)
        bias = sb("bias", [P, HG, BAND], into=mixer)
        prob = sb("prob", [P, 2, HG, BAND], into=mixer)
        pt_hi = sb("pt_hi", [P, 2, HG * P], f32r, into=mixer)
        pt_lo = sb("pt_lo", [P, 2, HG * P], f32r, into=mixer)
        ada = sb("ada", [P, 2, D], into=mixer)
        acc = sb("acc", [P, D], into=mixer)
        mixer.close()
        k_nat = prob[:, 0, :, :].rearrange("p h j -> p (h j)")[:, 0:NB * KV * HD]
        k_sq = prob[:, 1, :, :].rearrange("p h j -> p (h j)")[:, 0:NB * KV * HD]
        k_T = merged[:, 0:2, :]

        channel = ExitStack()
        g_hi = sb("g_hi", [P, FT, S], f32r, into=channel)
        g_lo = sb("g_lo", [P, FT, S], f32r, into=channel)
        channel.close()
        def hb(k):
            return (a_buf, y_buf)[k % 4 // 2][:, k % 2, :]

        par_rows = w_raw[:, 1, :, :].rearrange("p k n -> p (k n)")

        bank = [ctx.enter_context(nc.psum_tensor(f"bank{i}", [P, S], fp32)) for i in range(8)]
        SC, TB, OB, MB = (2, 3), (4, 5), 6, 7

        par_in, sink_in = sem("par_in"), sem("sink_in")
        c_in = sem("c_in")
        x_in = [sem(f"x_in{b}") for b in range(NB)]
        ada0_in = [sem(f"ada0_in{k}") for k in range(RING)]
        ada_in = [sem(f"ada_in{k}") for k in range(2)]
        w_in_slot = [sem(f"w_loaded{s}") for s in range(2)]
        out_dma = [sem(f"out_stored{s}") for s in range(2)]
        const_done = sem("const_done")
        dist_done = sem("dist_done")
        bias_done = sem("bias_done")
        hi_ready = sem("hi_ready")
        lo_ready = sem("lo_ready")
        units_done = sem("units_done")
        par_t, par_c = sem("par_transposed"), sem("par_copied")
        c_t, c_th = sem("c_transposed"), sem("c_tanh")
        x_sq = sem("x_squared")
        xd_done, xr_done = sem("x_diag"), sem("x_rstd_spread")
        r_copy, xr_pool = sem("x_rstd_copied"), sem("x_normed_by_pool")
        cb_done, pe_ada, mod_read, amp_done = sem("c_spread"), sem("ada_used_by_pe"), sem("mod_read"), sem("amp_done")
        xt_done, xt_out = sem("x_transposed"), sem("xt_copied")
        gemv_done, mod_done = sem("gemv_done"), sem("mod_summed")
        h_lo_pool = sem("h_low_by_pool")
        h_f, h_h, h_ready = sem("h_float"), sem("h_high"), sem("h_ready")
        var_ready, root_ready = sem("var_ready"), sem("root_ready")
        kn_ready, kt_done, kh_done, kl_done = sem("k_normed"), sem("k_transposed"), sem("k_high"), sem("k_low")
        g_act, g_dve = sem("drained_by_act"), sem("drained_by_dve")
        score_free, t_free, o_free, m_free = sem("score_free"), sem("t_free"), sem("o_free"), sem("m_free")
        mix_free = sem("mix_free")
        q_sq, q_hi, q_lo = sem("q_squared"), sem("q_high"), sem("q_low")
        ssq_done, s_done, t_done, pt_h, pv_done = (sem("q_sums"), sem("scores"), sem("p_transposed"),
                                                   sem("pt_high"), sem("pv"))
        v_staged, shift_ready, exp_done, p_ready = sem("v_staged"), sem("shift_ready"), sem("exp_done"), sem("p_ready")
        ma_done = sem("branch_a_gated")
        out_low = sem("outputs_of_low_values")
        m_hi_pool = sem("merged_high_by_pool")
        m_hi, m_lo, m_lo_dve = sem("merged_high"), sem("merged_low"), sem("merged_low_last")
        x2_done, x2_sq, sum_done, ss_done, diag_done, r_done = (sem("x2"), sem("x2_squared"), sem("x2_summed"),
                                                                sem("norm2_sums"), sem("diag"), sem("rstd_spread"))
        wo_half, x2_half, sq_half, sum_half = (sem("wo_half"), sem("x2_half"), sem("x2_half_squared"),
                                               sem("x2_half_summed"))
        t2_done, h2_h, h2_f = sem("h2_scaled"), sem("h2_high"), sem("h2_float")
        h2_ready, h2_ready_pool = sem("h2_ready"), sem("h2_ready_by_pool")
        a_free, b_free = sem("act_drained_ffn"), sem("dve_drained_ffn")
        conv_done, f_sq, z_done, f_th = sem("ffn_conv"), sem("ffn_squared"), sem("gelu_arg"), sem("gelu_tanh")
        ffn_tiles = sem("ffn_tiles")
        yt_done = sem("y_transposed")
        act_done, dve_done, pool_done = sem("act_steps"), sem("dve_steps"), sem("pool_steps")

        HS = S // 2
        WO_BANK = [2, 3, 0, 1, 4, 5]
        WO_HALVES = [(0, 6, 6), (0, 7, 7), (1, 6, 4), (1, 7, 5)]

        def half(c):
            return slice(c * HS, (c + 1) * HS)

        def wo_parts(k):
            if k < HT:
                return k_st[:, 0, k, :], k_st[:, 1, k, :]
            return h_hi[:, k, :], h_lo[:, k, :]

        def by_pool(m):
            return m < KT and m % 2 == 1

        def h2_signal(m):
            if by_pool(m):
                return h2_ready_pool, m // 2 + 1
            return h2_ready, m // 2 + 1 if m < KT else m - HT + 1

        def tb(f):
            return (a_buf, b_buf)[f % 4 // 2][:, f % 2, :]

        def at(i, per, n):
            return n if i is None else i * per + n

        TS = [[0, 1], [2, 3, 4], [5, 6, 7], [8, 9]]
        NT = 10
        STEPS, STEPS_UP = 36, 8

        block = ctx.enter_context(nc.Block())

        @block.sync
        def _(sp):
            def load(i, per, n, src):
                if n >= 2:
                    sp.wait_ge(lo_ready, at(i, 2 * per, 2 * n - 2))
                sp.dma_start(w_raw[:, n % 2, 0:src.shape[1], :], src).then_inc(w_in_slot[n % 2], 16)

            def parameters():
                rows = KT
                for src, n in ((b_ada, 6 * KT), (norm1_gain, KT), (norm2_gain, KT), (conv_w[0], 3 * KT)):
                    sp.dma_start(par_rows[rows:rows + n, 0:P],
                                 src.rearrange("a (f p) -> (a f) p", p=P)).then_inc(par_in, 16)
                    rows += n
                for r, src in enumerate((q_gain, k_gain)):
                    for a in range(2):
                        sp.dma_start(par_rows[rows + r:rows + r + 1, a * HD:(a + 1) * HD], src).then_inc(par_in, 16)
                sp.dma_start(par_rows[0:3 * FT, P:2 * P],
                             ffn_conv_w[0].rearrange("a (f p) -> (a f) p", p=P)).then_inc(par_in, 16)
                sp.dma_start(par_rows[3 * FT:4 * FT, P:2 * P],
                             ffn_conv_b.rearrange("a (f p) -> (a f) p", p=P)).then_inc(par_in, 16)
                sp.dma_start(sink_b[:, :], sink.to_broadcast([P, H])).then_inc(sink_in, 16)

            sp.dma_start(par_rows[0:KT, 0:P], c.rearrange("a (f p) -> (a f) p", p=P)).then_inc(c_in, 16)
            for b in range(NB):
                sp.dma_start(x_nat[:, b, :], x[0, b * P:(b + 1) * P, :]).then_inc(x_in[b], 16)
            for n in range(2 * KT):
                a, k = n // KT, n % KT
                m = n - RING
                if m in PE_ADA:
                    sp.wait_ge(pe_ada, PE_ADA.index(m) + 1)
                elif m >= 0:
                    sp.wait_ge(gemv_done, DVE_ADA.index(m) + 1)
                sp.dma_start(ada0[:, n % RING],
                             w_ada[0, k * P:(k + 1) * P, 0:2 * D].rearrange("p (s n) -> p s n", s=2)[
                                 :, :, a * (D // 2):(a + 1) * (D // 2)]).then_inc(ada0_in[n % RING], 16)
                if n == 3:
                    parameters()
                if n == 7:
                    load(None, 0, 0, wi[:, :, COL_K:COL_K + PC])
                if n == 9:
                    sp.wait_ge(par_t, 2)
                    load(None, 0, 1, wi[:, :, COL_V:COL_V + PC])
            with sp.Fori(1, KV + 1) as g1:
                g = g1 - 1
                for n in range(NM):
                    load(g, NM, P_MIX + n, wi[:, :, bass.ds(g1 * PC + (MIX[n] - PC), PC)])
                    for k in ([], [], [0, 1, 2, 3], [4, 5], [6, 7], [])[n]:
                        sp.wait_ge(gemv_done, g * KT + (G0 + k - 1))
                        sp.dma_start(ada[:, k % 2, :],
                                     w_ada[0, k * P:(k + 1) * P, bass.ds(g1 * D + D, D)]).then_inc(ada_in[k % 2], 16)
            for n in range(D // PC):
                load(None, 0, P_WO + n, wo[:, :, n * PC:(n + 1) * PC])
            with sp.Fori(1, FF // PC + 1) as j1:
                j = j1 - 1
                for n in range(2):
                    load(j, 2, P_UP + n, wu[:, :, bass.ds(j1 * PC + (n * FF - PC), PC)])
            with sp.Fori(1, 3) as i1:
                i = i1 - 1
                for n in range(6):
                    q, k0 = n // 3, 8 * (n % 3)
                    load(i, 6, P_DOWN + n, wd[:, k0:k0 + CH[n % 3], bass.ds(i1 * (2 * PC) + (q - 2) * PC, PC)])

        @block.gpsimd
        def _(pool):
            steps = Tally(pool, pool_done)

            def low(i, per, n, units=(0, 1)):
                for u in units:
                    pool.wait_ge(hi_ready, at(i, 2 * per, 2 * n + u + 1))
                    pool.tensor_tensor(w_lo[:, n % 2, u], w_raw[:, n % 2, :, u * P:(u + 1) * P],
                                       w_hi[:, n % 2, u], SUB).then_inc(lo_ready, 1)

            steps.link(pool.memset(ident[:, :], 0.0))
            pool.affine_select(out=ident[:, :], in_=ident[:, :], compare_op=ALU.not_equal, fill=1.0, base=0,
                               pattern=[[-1, P]], channel_multiplier=1).then_inc(const_done, 1)
            pool.memset(ones[:, :], 1.0).then_inc(const_done, 1)
            pool.iota(ndist[:, :], pattern=[[-1, BAND]], base=P, channel_multiplier=1,
                      allow_small_or_imprecise_dtypes=True).then_inc(const_done, 1)
            pool.wait_ge(dist_done, 1)
            steps.link(pool.affine_select(out=ndist[:, :], in_=ndist[:, :], compare_op=ALU.is_ge, fill=MASKED,
                                          base=2 * P, pattern=[[-1, BAND]], channel_multiplier=1))
            steps.link(pool.affine_select(out=ndist[:, :], in_=ndist[:, :], compare_op=ALU.is_ge, fill=MASKED,
                                          base=0, pattern=[[1, BAND]], channel_multiplier=-1))
            pool.wait_ge(r_copy, 1)
            for k in range(KT):
                pool.wait_ge(xt_out, k + 1)
                pool.tensor_tensor(hT[:, k, :], xT[:, k, :], b_buf[:, 0, :], MUL).then_inc(xr_pool, 1)
            low(None, 0, 0, (0,))
            for k in range(1, HT):
                pool.wait_ge(h_h, k + 1)
                pool.wait_ge(h_f, k + 1)
                pool.tensor_tensor(h_lo[:, k, :], hb(k), h_hi[:, k, :], SUB).then_inc(h_lo_pool, 1)
            pool.wait_ge(lo_ready, 2)
            low(None, 0, 1)
            pool.wait_ge(h_ready, HT + 1)
            for h in range(HG):
                slope = float(np.float32(2.0 ** (-8.0 * (h + 1) / H)))
                pool.tensor_scalar(bias[:, h, :], ndist[:, :], slope, 1.0, MUL, MUL).then_inc(bias_done, 1)
            low(None, 0, 2)
            with pool.Fori(0, KV) as g:
                for n in range(NM):
                    if n == 5:
                        pool.wait_ge(score_free, g * (NB * HG) + (NB * HG + 2))
                    low(g, NM, P_MIX + n + 1)
                    if n == 5:
                        pool.tensor_scalar(bias[:, :, :], bias[:, :, :], 2.0 ** (-8 * HG // H), 1.0,
                                           MUL, MUL).then_inc(bias_done, 1)
            pool.wait_ge(s_done, KV * NB * HG)
            for k in range(KT - 2):
                hi, lo = wo_parts(k)
                if k < HT:
                    pool.wait_ge(mix_free, k + 3)
                    pool.tensor_scalar(hi, merged[:, k, :], 1.0, 1.0, MUL, MUL).then_inc(m_hi_pool, 1)
                    pool.wait_ge(m_hi_pool, k + 1)
                else:
                    pool.wait_ge(m_hi, k - HT + 1)
                pool.tensor_tensor(lo, merged[:, k, :], hi, SUB).then_inc(m_lo, 1)
            for n in range(P_WO + 1, P_UP + 1):
                low(None, 0, n)
            for f in range(1, KT, 2):
                pool.wait_ge(h2_f, f // 2 + 1)
                pool.tensor_tensor(h_lo[:, f, half(0)], tb(f)[:, half(0)], h_hi[:, f, half(0)],
                                   SUB).then_inc(h2_ready_pool, 1)
            low(None, 0, P_UP + 1)
            with pool.Fori(0, FF // PC) as j:
                for n in range(2):
                    low(j, 2, P_UP + n + 2)
            for n in range(P_DOWN + 2, P_END):
                low(None, 0, n)

        @block.scalar
        def _(act):
            steps = Tally(act, act_done)

            def high(i, per, n, units=(0, 1)):
                act.wait_ge(w_in_slot[n % 2], at(i, 16 * per // 2, 16 * (n // 2) + 16))
                if n >= 2:
                    act.wait_ge(units_done, at(i, 2 * per, 2 * n - 2))
                for u in units:
                    act.activation(w_hi[:, n % 2, u], w_raw[:, n % 2, :, u * P:(u + 1) * P],
                                   ACT.Copy).then_inc(hi_ready, 1)

            act.wait_ge(c_t, 1)
            act.activation(c_act[:, 1, :], bank[5][:, 0:KT], ACT.Tanh, scale=0.5).then_inc(c_th, 1)
            def table_of_roots():
                act.activation(st[:, 5, 15:16], ones[:, 0:1], ACT.Sqrt)

            act.wait_ge(const_done, 2)
            table_of_roots()
            for b in range(NB):
                act.wait_ge(x_in[b], 16)
                act.activation(hT[:, 2 * b:2 * b + 2, :].rearrange("p k n -> p (k n)"), x_nat[:, b, :], ACT.Square,
                               accum_out=st[:, 0, b:b + 1]).then_inc(x_sq, 1)
            roots = 0

            def root(i, per, n, cols, src, dst):
                act.wait_ge(var_ready, at(i, per, n + 1))
                act.activation(st[:, dst, 0:cols], st[:, src, 0:cols], ACT.Sqrt).then_inc(root_ready, 1)

            root(None, 0, 0, NB, 1, 2)
            for m in range(KT):
                act.wait_ge(xt_done, m + 1)
                act.activation(xT[:, m, :], bank[m % 4][:, :], ACT.Copy).then_inc(xt_out, 1)
                if m == 3:
                    act.wait_ge(xr_done, 1)
                    act.activation(b_buf[:, 0, :], bank[4][:, :], ACT.Copy).then_inc(r_copy, 1)
            act.wait_ge(par_t, 2)
            for t, (r0, n) in enumerate(((0, ROWS1), (ROWS1, ROWS2))):
                act.activation(par[:, r0:r0 + n], bank[5][:, (t + 1) * P:(t + 1) * P + n], ACT.Copy).then_inc(par_c, 1)
            high(None, 0, 0)
            for k in range(KT):
                act.wait_ge(amp_done, k // HT + 1)
                act.wait_ge(xr_pool, k + 1)
                act.activation(h_hi[:, k, :], hT[:, k, :], ACT.Identity, bias=mod[:, k:k + 1],
                               scale=amp[:, 0, k:k + 1]).then_inc(h_h, 1)
                if k == HT - 1:
                    high(None, 0, 1)
            act.wait_ge(units_done, 2)
            act.wait_ge(h_ready, HT + 1)
            for b in range(NB):
                act.activation(k_nat[:, b * PC:(b + 1) * PC], bank[b][:, 0:PC], ACT.Copy).then_inc(g_act, 1)
            high(None, 0, 2)
            root(None, 0, 1, NB * KV, 1, 2)
            act.wait_ge(units_done, 4)
            act.activation(v_nat[:, 2, :], bank[6][:, 0:PC], ACT.Copy).then_inc(o_free, 1)
            for j in range(KV):
                act.wait_ge(score_free, j // 2 + 1)
                a = (j % 2) * HD
                for o in range(2):
                    act.activation(k_st[o * HD:(o + 1) * HD, 0, j, :], k_T[a:a + HD, j // 2, :],
                                   ACT.Copy).then_inc(kh_done, 1)

            with act.Fori(0, KV) as g:
                U = 2 * P_MIX

                def unit(n):
                    act.wait_ge(units_done, g * (2 * NM) + (U + n + 1))

                def query(u):
                    unit(u)
                    act.wait_ge(mix_free, g * 2 + 2)
                    act.activation(y_buf[:, u, :], bank[u][:, :], ACT.Copy).then_inc(g_act, 1)
                    act.wait_ge(g_act, g * 8 + (NB + u + 1))
                    for o in range(2):
                        r = slice(o * HD, (o + 1) * HD)
                        act.activation(q_st[r, 2 * u + o, :], y_buf[r, u, :], ACT.Copy).then_inc(q_hi, 1)

                def squares(u):
                    act.wait_ge(ssq_done, g * 2 + (u + 1))
                    act.activation(b_buf[:, u, :], bank[TB[u]][:, :], ACT.Square).then_inc(q_sq, 1)

                def conv_c(u):
                    unit(2 + u)
                    act.activation(a_buf[:, u, :], bank[u][:, :], ACT.Copy).then_inc(g_act, 1)

                def exps(b):
                    w = BAND if 0 < b < NB - 1 else 2 * P
                    act.wait_ge(shift_ready, g * NB + (b + 1))
                    for h in range(HG):
                        act.activation(prob[:, b % 2, h, 0:w], prob[:, b % 2, h, 0:w], ACT.Exp,
                                       bias=sm[:, 1, b, h:h + 1], accum_out=sm[:, 3, b, h:h + 1]).then_inc(exp_done, 1)
                    act.activation(sm[:, 4, b, :], sm[:, 2, b, :], ACT.Exp).then_inc(exp_done, 1)

                def turned_high(ts):
                    for t in ts:
                        act.wait_ge(t_done, g * NT + (t + 1))
                        act.activation(pt_hi[:, t % 2, :], bank[TB[t % 2]][:, :], ACT.Copy).then_inc(pt_h, 1)

                def heads_low(b):
                    act.wait_ge(pv_done, g * NB + (b + 1))
                    act.wait_ge(q_lo, g * HG + HG)
                    for o in range(2):
                        act.activation(y_buf[o * HD:(o + 1) * HD, :, b * P:(b + 1) * P],
                                       bank[OB][HD:P, :].rearrange("p (u o q) -> p u o q", u=2, o=2)[:, :, o, :],
                                       ACT.Copy).then_inc(out_low, 1)

                def gate(n):
                    unit(n)
                    if n >= 10:
                        act.wait_ge(ma_done, g * 2 + (n - 9))
                    act.activation(b_buf[:, n % 2, :], bank[n % 2][:, :], ACT.Tanh, scale=0.5).then_inc(g_act, 1)

                high(g, NM, P_MIX + 1, (0,))
                query(0)
                table_of_roots()
                high(g, NM, P_MIX + 1, (1,))
                squares(0)
                query(1)
                high(g, NM, P_MIX + 2)
                squares(1)
                conv_c(0)
                root(g, 1, 2, NB * HG, 1, 2)
                conv_c(1)
                high(g, NM, P_MIX + 3)
                exps(0)
                turned_high(TS[0])
                exps(1)
                high(g, NM, P_MIX + 4)
                heads_low(0)
                turned_high(TS[1])
                exps(2)
                high(g, NM, P_MIX + 5)
                heads_low(1)
                gate(8)
                turned_high(TS[2][:2])
                exps(3)
                turned_high(TS[2][2:])
                gate(9)
                high(g, NM, P_MIX + 6)
                heads_low(2)
                turned_high(TS[3])
                gate(10)
                heads_low(3)
                gate(11)

            act.wait_ge(units_done, 2 * P_WO)
            for k in range(HT, KT):
                act.wait_ge(mix_free, k + 3)
                act.activation(h_hi[:, k, :], merged[:, k, :], ACT.Copy).then_inc(m_hi, 1)
            table_of_roots()
            for n in range(D // PC):
                high(None, 0, P_WO + n + 1)
                for f in (2 * n, 2 * n + 1):
                    if f >= KT - 2:
                        continue
                    if f in (4, 5):
                        act.wait_ge(b_free, f - 3)
                    else:
                        act.wait_ge(x2_done, f + 1)
                    if f >= 2:
                        act.wait_ge(sum_done, max(f - 2, 1))
                    act.activation(b_buf[:, f % 2, :], xT[:, f, :],
                                   ACT.Square).then_inc(a_free if f in (2, 3) else x2_sq, 1)

            def square_half(i):
                c, f, _ = WO_HALVES[i]
                act.wait_ge(x2_half, i + 1)
                act.wait_ge(sum_done, f - 2)
                act.activation(b_buf[:, f % 2, half(c)], xT[:, f, half(c)], ACT.Square).then_inc(sq_half, 1)

            def h2_high(m):
                c, f = m // KT, m % KT
                act.wait_ge(t2_done, m + 1)
                act.activation(h_hi[:, f, half(c)], tb(f)[:, half(c)], ACT.Identity,
                               bias=mod[:, 3 * KT + f:3 * KT + f + 1]).then_inc(h2_h, 1)
                if by_pool(m):
                    act.activation(tb(f)[:, half(c)], tb(f)[:, half(c)], ACT.Identity,
                                   bias=mod[:, 3 * KT + f:3 * KT + f + 1]).then_inc(h2_f, 1)

            square_half(0)
            square_half(1)
            root(None, 0, 2 + KV, 2, 1, 2)
            square_half(2)
            for m in range(2 * KT):
                h2_high(m)
                if m == 1:
                    square_half(3)
                if m == 4:
                    root(None, 0, 3 + KV, 2, 1, 2)
                if m in (5, 7):
                    high(None, 0, P_UP + 1, (m // 2 - 2,))

            with act.Fori(0, FF // PC) as j:
                U = 2 * P_UP
                for u in range(2):
                    act.wait_ge(units_done, j * 4 + (U + u + 1))
                    act.activation(pad[u][:, 1:S + 1], bank[2 + u][:, :], ACT.Copy).then_inc(a_free, 1)
                high(j, 2, P_UP + 2)
                for u in range(2):
                    act.wait_ge(conv_done, j * 2 + (u + 1))
                    act.activation(b_buf[:, u, :], a_buf[:, u, :], ACT.Square).then_inc(f_sq, 1)
                for u in range(2):
                    act.wait_ge(z_done, j * 2 + (u + 1))
                    act.activation(b_buf[:, u, :], b_buf[:, u, :], ACT.Tanh,
                                   scale=GELU_C * GELU_S).then_inc(f_th, 1)
                high(j, 2, P_UP + 3)

            def store(q):
                stage = stages[q % 2]
                if q >= 2:
                    act.wait_ge(out_dma[q % 2], 32)
                for u in range(2):
                    act.wait_ge(yt_done, 2 * q + u + 1)
                    act.activation(stage[:, :, u * P:(u + 1) * P],
                                   bank[4 + 2 * (q % 2) + u][:, :].rearrange("p (b n) -> p b n", b=NB),
                                   ACT.Copy).then_inc(a_free, 1)
                    act.wait_ge(a_free, 2 + 2 * FF // PC + 2 * q + u + 1)
                    act.dma_start(out_v[:, :, q * PC + u * P:q * PC + (u + 1) * P],
                                  stage[:, :, u * P:(u + 1) * P]).then_inc(out_dma[q % 2], 16)

            stages = [b_buf[:, :, :].rearrange("p u s -> p (u s)").rearrange("p (b n) -> p b n", b=NB),
                      pad_f[:, 0:2 * S].rearrange("p (b n) -> p b n", b=NB)]
            for n in range(P_DOWN, P_END):
                if n + 2 < P_END:
                    high(None, 0, n + 2)
                if n == P_DOWN + 4:
                    store(0)
                if n == P_DOWN + 6:
                    store(1)
                if n == P_DOWN + 10:
                    store(2)
            store(3)
            for s in range(2):
                act.wait_ge(out_dma[s], 64)

        @block.tensor
        def _(pe):
            def three(dst, w_h, w_l, rhs_hi, rhs_lo, first, last):
                pe.matmul(dst, w_h, rhs_hi, start=first, stop=False)
                pe.matmul(dst, w_h, rhs_lo, start=False, stop=False)
                return pe.matmul(dst, w_l, rhs_hi, start=False, stop=last)

            pe.wait_ge(const_done, 1)
            pe.wait_ge(c_in, 16)
            pe.transpose(bank[5][:, 0:KT], par_rows[0:KT, 0:P], ident[0:KT, 0:KT]).then_inc(c_t, 1)
            for b in range(NB):
                pe.wait_ge(x_in[b], 16)
            for m in range(KT):
                if m >= 4:
                    pe.wait_ge(xt_out, m - 3)
                for b in range(NB):
                    mm = pe.transpose(bank[m % 4][:, b * P:(b + 1) * P], x_nat[:, b, m * P:(m + 1) * P], ident[:, :])
                mm.then_inc(xt_done, 1)
                if m == 3:
                    pe.wait_ge(const_done, 2)
                    pe.wait_ge(xd_done, NB)
                    pe.matmul(bank[4][:, :], ones[:, :], y_buf[:, 1, :], start=True, stop=True).then_inc(xr_done, 1)

            def ada_product(n):
                pe.wait_ge(ada0_in[n % RING], 16 * (n // RING) + 16)
                for s in range(2):
                    mm = pe.matmul(bank[6 + s][:, :], c_b[:, :], ada0[:, n % RING, s, :], start=True, stop=True)
                mm.then_inc(pe_ada, 1)

            def mod_turn(a):
                pe.wait_ge(gemv_done, sum(n < (a + 1) * KT for n in DVE_ADA))
                pe.wait_ge(r_copy, 1)
                for s in range(2):
                    for f in range(HT):
                        mm = pe.transpose(bank[4 + s][:, f * P:(f + 1) * P], acc0[:, a, s, f * P:(f + 1) * P],
                                          ident[:, :])
                    mm.then_inc(mod_done, 1)

            pe.wait_ge(par_in, 16 * 10)
            for t, n in enumerate((ROWS1, ROWS2)):
                pe.transpose(bank[5][:, (t + 1) * P:(t + 1) * P + n], par_rows[0:n, t * P:(t + 1) * P],
                             ident[0:n, 0:n]).then_inc(par_t, 1)

            def token_major(n, ks, bs=range(NB)):
                for k in ks:
                    if 1 <= k < HT:
                        pe.wait_ge(h_lo_pool, k)
                    else:
                        pe.wait_ge(h_ready, max(k - HT + 2, 1))
                    for b in bs:
                        dst = bank[4 * n + b][:, 0:PC].rearrange("p (u n) -> p u n", u=2)
                        t = slice(b * P, (b + 1) * P)
                        mm = three(dst, h_hi[:, k, t], h_lo[:, k, t], w_hi[:, n, :, k, :], w_lo[:, n, :, k, :],
                                   k == 0, k == KT - 1)
                        if k == KT - 1 and (n, b) in ((0, 2), (0, 3), (1, 3), (1, 1)):
                            mm.then_inc(units_done, 1)

            pe.wait_ge(par_c, 2)
            mod_turn(0)
            pe.wait_ge(cb_done, 1)
            ada_product(PE_ADA[0])
            pe.wait_ge(lo_ready, 2)
            token_major(0, range(HT))
            pe.wait_ge(lo_ready, 4)
            pe.wait_ge(mod_read, 1)
            pe.wait_ge(gemv_done, KT + 1)
            token_major(1, range(2), (2, 3))
            mod_turn(1)
            token_major(1, range(2, HT), (2, 3))
            token_major(0, range(HT, KT))
            token_major(1, range(HT, KT), (2, 3))
            token_major(1, range(KT), (0, 1))
            pe.wait_ge(kn_ready, 1)
            for f in range(2):
                for b in range(NB):
                    mm = pe.transpose(bank[SC[f]][:, b * P:(b + 1) * P],
                                      k_nat[:, b * PC + f * P:b * PC + (f + 1) * P], ident[:, :])
                mm.then_inc(kt_done, 1)

            with pe.Fori(0, KV) as g:
                def unit_waits(n):
                    pe.wait_ge(lo_ready, g * (2 * NM) + (2 * P_MIX + n + 1))
                    if n in (6, 7, 8, 9):
                        pe.wait_ge(g_dve, g * 4 + (n - 5))
                    else:
                        pe.wait_ge(g_act, g * 8 + {0: 3, 1: 4, 2: 5, 3: 6, 4: 7, 5: 8, 10: 9, 11: 10}[n])

                def unit_half(n, a):
                    s, u = (n // 2) % 2, n % 2
                    for k in range(4 * a, 4 * a + 4):
                        mm = three(bank[u][:, :], w_hi[:, s, u, k, :], w_lo[:, s, u, k, :],
                                   h_hi[:, k, :], h_lo[:, k, :], k == 0, k == KT - 1)
                    if a:
                        mm.then_inc(units_done, 1)

                def query_turn(u):
                    pe.wait_ge(g_act, g * 8 + (NB + u + 1))
                    pe.wait_ge(t_free, g * NT + 2)
                    for b in range(NB):
                        mm = pe.transpose(bank[TB[u]][:, b * P:(b + 1) * P], y_buf[:, u, b * P:(b + 1) * P],
                                          ident[:, :])
                    mm.then_inc(ssq_done, 1)

                def scores(b, hs):
                    j0, j1 = max(b - 1, 0) * P, min(b + 2, NB) * P
                    for h in hs:
                        pe.wait_ge(q_lo, g * HG + (h + 1))
                        pe.wait_ge(score_free, g * (NB * HG) + (b * HG + h + 1))
                        dst = bank[SC[h % 2]][:, 0:j1 - j0]
                        for p in range(2):
                            mm = pe.matmul(dst, q_st[:, h, b * P:(b + 1) * P],
                                           k_st[:, p, bass.ds(g, 1), j0:j1].rearrange("p a n -> p (a n)"),
                                           start=(p == 0), stop=(p == 1))
                        mm.then_inc(s_done, 1)

                def turn(b, i):
                    t = TS[b][i]
                    pe.wait_ge(p_ready, g * (NB * HG) + (b * HG + HG))
                    pe.wait_ge(t_free, g * NT + (t + 1))
                    for h in range(HG):
                        mm = pe.transpose(bank[TB[t % 2]][:, h * P:(h + 1) * P],
                                          prob[:, b % 2, h, i * P:(i + 1) * P], ident[:, :])
                    mm.then_inc(t_done, 1)

                def values(b, i):
                    t = TS[b][i]
                    pe.wait_ge(t_free, g * NT + (t + 3))
                    if i == 0:
                        pe.wait_ge(v_staged, g + 1)
                        pe.wait_ge(o_free, g * (2 * NB) + (2 * b + 1))
                    kb = max(b - 1, 0) + i
                    last = i == len(TS[b]) - 1
                    hi_lo = (bank[OB][:, :], v_st[:, kb], pt_hi[:, t % 2, :])
                    hi = (bank[OB][0:HD, :], v_st[:, kb, 0, :], pt_lo[:, t % 2, :])
                    for n, args in enumerate((hi, hi_lo) if last else (hi_lo, hi)):
                        mm = pe.matmul(*args, start=(i == 0 and n == 0), stop=(last and n == 1))
                    if last:
                        mm.then_inc(pv_done, 1)

                def ada_turn(a):
                    pe.wait_ge(gemv_done, g * KT + (G0 + KT))
                    pe.wait_ge(m_free, g * 2 + (a + 1))
                    for f in range(HT):
                        mm = pe.transpose(bank[MB][:, f * P:(f + 1) * P],
                                          acc[:, (a * HT + f) * P:(a * HT + f + 1) * P], ident[:, :])
                    mm.then_inc(mod_done, 1)

                SCORE_SLOT, TURN_SLOT = (6, 9, 13, 16), (11, 14, 18, 21)
                for slot in range(4 * NM):
                    if slot in (3, 5):
                        query_turn((slot - 3) // 2)
                    for b in range(NB):
                        r = slot - TURN_SLOT[b]
                        if r == 0:
                            turn(b, 0)
                            turn(b, 1)
                        if r == 1:
                            values(b, 0)
                            if len(TS[b]) == 3:
                                turn(b, 2)
                            values(b, 1)
                        if r == 2 and len(TS[b]) == 3:
                            values(b, 2)
                    for b in range(NB):
                        if slot == SCORE_SLOT[b]:
                            scores(b, (0, 1))
                        if slot == SCORE_SLOT[b] + 1:
                            scores(b, (2, 3))
                    if slot in (13, 17):
                        ada_turn((slot - 13) // 4)
                    if slot % 2 == 0:
                        unit_waits(slot // 2)
                    unit_half(slot // 2, slot % 2)

            def tile_k(n, u, k, dst, rhs, k_off, first, last, t=slice(0, S)):
                hi, lo = rhs(k_off + k)
                return three(bank[dst][:, t], w_hi[:, n % 2, u, k, :], w_lo[:, n % 2, u, k, :],
                             hi[:, t], lo[:, t], first, last)

            def h_parts(k):
                return h_hi[:, k, :], h_lo[:, k, :]

            def g_parts(k):
                return g_hi[:, k, :], g_lo[:, k, :]

            def pair(i, per, n, banks, rhs, kn=8, k_off=0, first=True, last=True, between=None):
                for u in range(2):
                    pe.wait_ge(lo_ready, at(i, 2 * per, 2 * n + u + 1))
                    for k in range(kn):
                        mm = tile_k(n, u, k, banks[u], rhs, k_off, first and k == 0, last and k == kn - 1)
                        if between and (u, k) == (1, 3):
                            between()
                    mm.then_inc(units_done, 1)

            pe.wait_ge(score_free, 2 + KV * NB * HG)
            pe.wait_ge(lo_ready, 2 * P_WO + 2)
            for k in range(KT):
                pe.wait_ge(*((m_lo, k + 1) if k < KT - 2 else (m_lo_dve, k + 3 - KT)))
                for u in range(2):
                    mm = tile_k(P_WO, u, k, WO_BANK[u], wo_parts, 0, k == 0, k == KT - 1)
                    if k == KT - 1:
                        mm.then_inc(units_done, 1)
            pe.wait_ge(g_act, NB + 8 * KV)
            pe.wait_ge(m_free, 2 * KV + 1)
            for n in range(1, D // PC - 1):
                pair(None, 0, P_WO + n, WO_BANK[2 * n:2 * n + 2], wo_parts)

            def sum_turn(c):
                pe.wait_ge(sum_half, 2 * c + 2)
                for b in range(2):
                    mm = pe.transpose(bank[6 + c][:, b * P:(b + 1) * P],
                                      y_buf[:, 0, c * HS + b * P:c * HS + (b + 1) * P], ident[:, :])
                mm.then_inc(ss_done, 1)

            def spread(c):
                pe.wait_ge(diag_done, 2 * c + 2)
                pe.matmul(bank[1 - c][:, 0:HS], ones[:, :], y_buf[:, 1, half(c)], start=True,
                          stop=True).then_inc(r_done, 1)

            for i, (c, f, dst) in enumerate(WO_HALVES):
                if c == 1:
                    pe.wait_ge(b_free, 2)
                pe.wait_ge(lo_ready, 2 * P_WO + f + 1)
                for k in range(KT):
                    mm = tile_k(P_WO + f // 2, f % 2, k, dst, wo_parts, 0, k == 0, k == KT - 1, half(c))
                    if (i, k) == (2, 4):
                        sum_turn(0)
                    if (i, k) == (3, 4):
                        spread(0)
                mm.then_inc(units_done if c else wo_half, 1)

            pe.wait_ge(a_free, 2)
            pe.wait_ge(lo_ready, 2 * P_UP + 2)
            for c in range(2):
                for k in range(KT):
                    pe.wait_ge(*h2_signal(c * KT + k))
                    for u in range(2):
                        mm = tile_k(P_UP, u, k, 2 + u, h_parts, 0, k == 0, k == KT - 1, half(c))
                        if c == 1 and k == KT - 1:
                            mm.then_inc(units_done, 1)
                    if (c, k) == (0, 1):
                        sum_turn(1)
                    if (c, k) == (0, 5):
                        spread(1)

            with pe.Fori(0, FF // PC - 1) as j:
                pe.wait_ge(b_free, j * 2 + 2)
                pair(j, 2, P_UP + 1, (4, 5), h_parts)
                pe.wait_ge(a_free, j * 2 + 4)
                pair(j, 2, P_UP + 2, (2, 3), h_parts)
            pe.wait_ge(b_free, 2 * (FF // PC))
            pair(None, 0, P_DOWN - 1, (4, 5), h_parts)

            with pe.Fori(0, 2) as i:
                def turn_out(q, u):
                    pe.wait_ge(ffn_tiles, i * 4 + (FT + 2 * q + u + 1))
                    pe.wait_ge(a_free, i * 4 + (2 + FT - 2 + 2 * q))
                    for b in range(NB):
                        mm = pe.transpose(bank[4 + 2 * q + u][:, b * P:(b + 1) * P],
                                          (a_buf, y_buf)[q][:, u, b * P:(b + 1) * P], ident[:, :])
                    mm.then_inc(yt_done, 1)

                for q in range(2):
                    for cc in range(3):
                        if cc == 0:
                            pe.wait_ge(ffn_tiles, i * 4 + (FT - 2 + 2 * q))
                        if cc == 2:
                            pe.wait_ge(ffn_tiles, FT)
                        between = None
                        if cc == 2:
                            def between(q=q):
                                turn_out(q, 0)
                        elif (q, cc) == (1, 0):
                            def between():
                                turn_out(0, 1)
                        pair(i, 6, P_DOWN + 3 * q + cc, (2 * q, 2 * q + 1), g_parts, kn=CH[cc], k_off=8 * cc,
                             first=cc == 0, last=cc == 2, between=between)
                turn_out(1, 1)

        @block.vector
        def _(dve):
            steps = Tally(dve, dve_done)

            def rsqrt(i, per, n, cols, ss, scale, dst, fold=1.0):
                variance(cols, ss, scale)
                from_root(i, per, n, cols, dst, fold)

            def variance(cols, ss, scale):
                dve.tensor_scalar(st[:, 1, 0:cols], ss, scale, EPS, MUL, ADD).then_inc(var_ready, 1)

            def from_root(i, per, n, cols, dst, fold=1.0):
                v, s, r, t = (st[:, m, 0:cols] for m in (1, 2, 3, 4))
                dve.wait_ge(root_ready, at(i, per, n + 1))
                steps.link(dve.reciprocal(r, s))
                steps.link(dve.scalar_tensor_tensor(t, v, -0.5 * fold, r, MUL, MUL))
                steps.link(dve.tensor_tensor(t, t, r, MUL))
                steps.link(dve.scalar_tensor_tensor(dst, t, 1.5 * fold, r, ADD, MUL))

            for u in range(2):
                dve.memset(pad_f[:, u * (S + 2):(u + 1) * (S + 2)], 0.0).then_inc(mix_free, 1)
            dve.wait_ge(const_done, 3)
            steps.link(dve.tensor_scalar(a_buf[:, 0, 0:BAND], ndist[:, :], -1.0, None, MUL))
            dve.tensor_tensor(ndist[:, :], ndist[:, :], a_buf[:, 0, 0:BAND], ALU.min).then_inc(dist_done, 1)
            dve.wait_ge(c_th, 1)
            steps.link(dve.scalar_tensor_tensor(c_act[:, 0, :], c_act[:, 1, :], 1.0, bank[5][:, 0:KT], ADD, MUL))
            steps.link(dve.tensor_scalar(c_act[:, 0, :], c_act[:, 0, :], 0.5, None, MUL))
            dve.tensor_scalar(c_b[:, :], ones[:, :], c_act[:, 0, 0:1], 1.0 / P, MUL, MUL).then_inc(cb_done, 1)
            dve.wait_ge(x_sq, NB)
            rsqrt(None, 0, 0, NB, st[:, 0, 0:NB], 1.0 / D, st[:, 5, 0:NB])
            for b in range(NB):
                dve.tensor_scalar(y_buf[:, 1, b * P:(b + 1) * P], ident[:, :], st[:, 5, b:b + 1], None,
                                  MUL).then_inc(xd_done, 1)

            def gemv0(n):
                a, k = n // KT, n % KT
                i = DVE_ADA.index(n)
                dve.wait_ge(ada0_in[n % RING], 16 * (n // RING) + 16)
                if n == 0:
                    dve.tensor_scalar(acc0[:, a], ada0[:, 0], c_act[:, 0, 0:1], None, MUL).then_inc(gemv_done, 1)
                elif n - 1 in PE_ADA:
                    dve.wait_ge(pe_ada, 1)
                    for s in range(2):
                        dve.scalar_tensor_tensor(acc0[:, a, s], ada0[:, n % RING, s], c_act[:, 0, k:k + 1],
                                                 bank[6 + s][:, :], MUL, ADD).then_inc((mod_read, gemv_done)[s], 1)
                else:
                    if n - 2 in PE_ADA:
                        dve.wait_ge(mod_read, 1)
                    dve.wait_ge(gemv_done, i)
                    dve.scalar_tensor_tensor(acc0[:, a], ada0[:, n % RING], c_act[:, 0, k:k + 1], acc0[:, a],
                                             MUL, ADD).then_inc(gemv_done, 1)

            def mods(a):
                for s in range(2):
                    dve.wait_ge(mod_done, 2 * a + s + 1)
                    steps.inc(dve.tensor_reduce(mod[:, s * KT + a * HT:s * KT + (a + 1) * HT],
                                                bank[4 + s][:, :].rearrange("p (f n) -> p f n", n=P), AX.X, ADD))
                dve.wait_ge(dve_done, steps.n)
                m2, b2 = (t.rearrange("p (s k) -> p s k", s=2)[:, :, a * HT:(a + 1) * HT]
                          for t in (mod[:, 0:2 * KT], par[:, PA_B:PA_B + 2 * KT]))
                dve.wait_ge(par_c, 2)
                steps.link(dve.tensor_tensor(m2, m2, b2, ADD))
                dve.scalar_tensor_tensor(amp[:, 0, a * HT:(a + 1) * HT], mod[:, KT + a * HT:KT + (a + 1) * HT], 1.0,
                                         par[:, PA_G1 + a * HT:PA_G1 + (a + 1) * HT], ADD, MUL).then_inc(amp_done, 1)
                dve.wait_ge(amp_done, a + 1)

            def modulated(k):
                dve.wait_ge(xr_pool, k + 1)
                if k >= 4:
                    if k == 4:
                        dve.wait_ge(h_ready, 1)
                    else:
                        dve.wait_ge(h_lo_pool, k - 4)
                dve.tensor_scalar(hb(k), hT[:, k, :], amp[:, 0, k:k + 1], mod[:, k:k + 1], MUL, ADD).then_inc(h_f, 1)

            def h_low(k):
                dve.wait_ge(h_f, k + 1)
                dve.wait_ge(h_h, k + 1)
                dve.tensor_tensor(h_lo[:, k, :], hb(k), h_hi[:, k, :], SUB).then_inc(h_ready, 1)

            for n in range(KT):
                gemv0(n)
            mods(0)
            for k in range(HT):
                modulated(k)
                if k == 0:
                    dve.wait_ge(hi_ready, 2)
                    dve.tensor_tensor(w_lo[:, 0, 1], w_raw[:, 0, :, P:2 * P], w_hi[:, 0, 1], SUB).then_inc(lo_ready, 1)
                    h_low(0)
            for n in DVE_ADA[KT:]:
                gemv0(n)
            mods(1)
            for k in range(HT, KT):
                modulated(k)
                if k > HT:
                    h_low(k - 1)
            h_low(KT - 1)
            dve.wait_ge(g_act, NB)
            steps.link(dve.tensor_tensor(k_sq, k_nat, k_nat, MUL))
            steps.link(dve.tensor_reduce(st[:, 0, :], k_sq.rearrange("p (a d) -> p a d", d=HD), AX.X, ADD))
            rsqrt(None, 0, 1, NB * KV, st[:, 0, 0:NB * KV], 1.0 / HD, st[:, 6, :])
            dve.tensor_tensor(k_nat.rearrange("p (a d) -> p a d", d=HD), k_nat.rearrange("p (a d) -> p a d", d=HD),
                              st[:, 6, :].unsqueeze(2).to_broadcast([P, NB * KV, HD]), MUL).then_inc(kn_ready, 1)
            dve.wait_ge(units_done, 4)
            for b, done in ((0, t_free), (1, t_free), (3, m_free)):
                dve.tensor_copy(v_nat[:, b, :], bank[4 + b][:, 0:PC]).then_inc(done, 1)
            for f in range(2):
                dve.wait_ge(kt_done, f + 1)
                dve.tensor_scalar(k_T[:, f, :], bank[SC[f]][:, :], par[:, PA_KG:PA_KG + 1], par[:, PA_QG:PA_QG + 1],
                                  MUL, MUL).then_inc(score_free, 1)
            dve.wait_ge(score_free, 2)
            for j in range(KV):
                a = (j % 2) * HD
                dve.wait_ge(kh_done, 2 * j + 2)
                for o in range(2):
                    dve.tensor_tensor(k_st[o * HD:(o + 1) * HD, 1, j, :], k_T[a:a + HD, j // 2, :],
                                      k_st[a:a + HD, 0, j, :], SUB).then_inc(kl_done, 1)
            dve.wait_ge(o_free, 1)
            dve.wait_ge(m_free, 1)
            dve.wait_ge(t_free, 2)
            dve.wait_ge(kl_done, 2 * KV)
            dve.wait_ge(sink_in, 16)

            with dve.Fori(0, KV) as g:
                steps.enter(g, STEPS)

                def gemv(k):
                    dve.wait_ge(ada_in[k % 2], g * (8 * KT) + (16 * (k // 2) + 16))
                    if k == 0:
                        ins = dve.tensor_scalar(acc[:, :], ada[:, 0, :], c_act[:, 0, 0:1], None, MUL)
                    else:
                        dve.wait_ge(gemv_done, g * KT + (G0 + k))
                        ins = dve.scalar_tensor_tensor(acc[:, :], ada[:, k % 2, :], c_act[:, 0, k:k + 1], acc[:, :],
                                                       MUL, ADD)
                    ins.then_inc(gemv_done, 1)

                def stage_values():
                    v = v_nat[:, :, bass.ds(g * HD, HD)]
                    steps.link(dve.tensor_scalar(v_st[:, :, 0, :], v, 1.0, None, MUL))
                    dve.tensor_tensor(v_st[:, :, 1, :], v, v_st[:, :, 0, :], SUB).then_inc(v_staged, 1)

                def query_low(u):
                    dve.wait_ge(q_hi, g * HG + (2 * u + 2))
                    for o in range(2):
                        r, w = slice(o * HD, (o + 1) * HD), slice((1 - o) * HD, (2 - o) * HD)
                        dve.tensor_tensor(q_st[w, 2 * u + o, :], y_buf[r, u, :], q_st[r, 2 * u + o, :],
                                          SUB).then_inc(q_lo, 1)

                def query_sums(u):
                    dve.wait_ge(q_sq, g * 2 + (u + 1))
                    steps.link(dve.tensor_reduce(st[:, 0, :].rearrange("p (b h) -> p b h", b=NB)[:, :, 2 * u:2 * u + 2],
                                                 b_buf[:, u, :].rearrange("p (b h d) -> p b h d", b=NB, h=2),
                                                 AX.X, ADD))

                def query_norm():
                    rsqrt(g, 1, 2, NB * HG, st[:, 0, :], 1.0 / HD, sm[:, 6, :, :].rearrange("p b h -> p (b h)"), RS)

                def ada_sums(a):
                    dve.wait_ge(mod_done, g * 2 + (4 + a + 1))
                    dve.tensor_reduce(st[:, 7, a * HT:(a + 1) * HT],
                                      bank[MB][:, :].rearrange("p (f n) -> p f n", n=P), AX.X, ADD).then_inc(m_free, 1)

                def take(b, hs):
                    w = P * len(TS[b])
                    c0 = P if b == 0 else 0
                    for h in hs:
                        dve.wait_ge(s_done, g * (NB * HG) + (b * HG + h + 1))
                        if b == 0 and h == 0:
                            dve.wait_ge(bias_done, g + HG)
                        dve.scalar_tensor_tensor(prob[:, b % 2, h, 0:w], bank[SC[h % 2]][:, 0:w], sm[:, 6, b, h:h + 1],
                                                 bias[:, h, c0:c0 + w], MUL, ADD).then_inc(score_free, 1)

                def shift(b):
                    w = P * len(TS[b])
                    dve.wait_ge(score_free, g * (NB * HG) + (b * HG + HG + 2))
                    steps.link(dve.tensor_reduce(sm[:, 0, b, :], prob[:, b % 2, :, 0:w], AX.X, MAX))
                    steps.link(dve.tensor_tensor(sm[:, 0, b, :], sm[:, 0, b, :], sink_b[:, bass.ds(g * HG, HG)], MAX))
                    steps.link(dve.tensor_scalar(sm[:, 1, b, :], sm[:, 0, b, :], -1.0, None, MUL))
                    dve.tensor_tensor(sm[:, 2, b, :], sm[:, 1, b, :], sink_b[:, bass.ds(g * HG, HG)],
                                      ADD).then_inc(shift_ready, 1)

                def normalise(b):
                    w = P * len(TS[b])
                    dve.wait_ge(exp_done, g * (NB * (HG + 1)) + (b + 1) * (HG + 1))
                    steps.link(dve.tensor_tensor(sm[:, 5, b, :], sm[:, 3, b, :], sm[:, 4, b, :], ADD))
                    steps.link(dve.reciprocal(sm[:, 5, b, :], sm[:, 5, b, :]))
                    for h in range(HG):
                        dve.tensor_scalar(prob[:, b % 2, h, 0:w], prob[:, b % 2, h, 0:w], sm[:, 5, b, h:h + 1], None,
                                          MUL).then_inc(p_ready, 1)

                def turned_low(ts):
                    for t in ts:
                        dve.wait_ge(pt_h, g * NT + (t + 1))
                        dve.tensor_tensor(pt_lo[:, t % 2, :], bank[TB[t % 2]][:, :], pt_hi[:, t % 2, :],
                                          SUB).then_inc(t_free, 1)

                def heads_out(b):
                    dve.wait_ge(out_low, g * (2 * NB) + (2 * b + 2))
                    for o in range(2):
                        dst = y_buf[o * HD:(o + 1) * HD, :, b * P:(b + 1) * P]
                        by_parity = bank[OB][0:HD, :].rearrange("p (u o q) -> p u o q", u=2, o=2)
                        dve.tensor_tensor(dst, by_parity[:, :, o, :],
                                          dst, ADD).then_inc(o_free, 1)

                def conv_in(u):
                    dve.wait_ge(units_done, g * (2 * NM) + (2 * P_MIX + 4 + u + 1))
                    dve.wait_ge(g_act, g * 8 + (NB + 3 + u))
                    dve.tensor_tensor(pad[u][:, 1:S + 1], bank[u][:, :], a_buf[:, u, :], MUL).then_inc(g_dve, 1)

                def taps(u):
                    def w(tap):
                        return par[:, bass.ds(g * 2 + (PA_CW + tap * KT + u), 1)]
                    dve.wait_ge(g_dve, g * 4 + (u + 1))
                    steps.link(dve.tensor_scalar(a_buf[:, u, :], pad[u][:, 0:S], w(0), None, MUL))
                    for tap in (1, 2):
                        steps.link(dve.scalar_tensor_tensor(a_buf[:, u, :], pad[u][:, tap:tap + S], w(tap),
                                                            a_buf[:, u, :], MUL, ADD))

                def conv_out(u):
                    dve.wait_ge(units_done, g * (2 * NM) + (2 * P_MIX + 6 + u + 1))
                    dve.scalar_tensor_tensor(a_buf[:, u, :], bank[u][:, :], 0.5, a_buf[:, u, :],
                                             MUL, MUL).then_inc(g_dve, 1)

                def gate_a(u):
                    dve.wait_ge(g_dve, g * 4 + (u + 3))
                    dve.wait_ge(g_act, g * 8 + (NB + 5 + u))
                    dve.scalar_tensor_tensor(a_buf[:, u, :], b_buf[:, u, :], 1.0, a_buf[:, u, :],
                                             ADD, MUL).then_inc(ma_done, 1)

                def merge(u):
                    dve.wait_ge(g_act, g * 8 + (NB + 7 + u))
                    dve.wait_ge(ma_done, g * 2 + (u + 1))
                    steps.link(dve.scalar_tensor_tensor(b_buf[:, u, :], b_buf[:, u, :], 1.0, y_buf[:, u, :], ADD, MUL))
                    dve.scalar_tensor_tensor(merged[:, bass.ds(g * 2 + u, 1), :].rearrange("p a n -> p (a n)"),
                                             b_buf[:, u, :], 0.5, a_buf[:, u, :], MUL, ADD).then_inc(mix_free, 1)

                gemv(0)
                gemv(1)
                stage_values()
                query_low(0)
                gemv(2)
                gemv(3)
                query_sums(0)
                query_low(1)
                query_sums(1)
                query_norm()
                take(0, (0, 1))
                gemv(4)
                take(0, (2, 3))
                gemv(5)
                shift(0)
                gemv(6)
                gemv(7)
                take(1, (0, 1))
                normalise(0)
                conv_in(0)
                take(1, (2, 3))
                shift(1)
                turned_low(TS[0])
                conv_in(1)
                taps(0)
                normalise(1)
                heads_out(0)
                take(2, (0, 1))
                conv_out(0)
                turned_low(TS[1][:2])
                take(2, (2, 3))
                shift(2)
                turned_low(TS[1][2:])
                taps(1)
                ada_sums(0)
                conv_out(1)
                take(3, (0, 1))
                normalise(2)
                take(3, (2, 3))
                shift(3)
                heads_out(1)
                turned_low(TS[2][:2])
                gate_a(0)
                turned_low(TS[2][2:])
                ada_sums(1)
                normalise(3)
                gate_a(1)
                heads_out(2)
                turned_low(TS[3])
                heads_out(3)
                dve.wait_ge(m_free, g * 2 + 3)
                steps.link(dve.tensor_tensor(mod[:, bass.ds(g * KT + 2 * KT, KT)], st[:, 7, 0:KT],
                                             par[:, bass.ds(g * KT + (PA_B + 2 * KT), KT)], ADD))
                dve.wait_ge(o_free, g * (2 * NB) + (2 * NB + 1))
                merge(0)
                merge(1)
                steps.leave(KV)

            steps.link(dve.scalar_tensor_tensor(amp[:, 1, :], mod[:, 4 * KT:5 * KT], 1.0, par[:, PA_G2:PA_G2 + KT],
                                                ADD, MUL))
            for k in range(KT - 2, KT):
                dve.wait_ge(m_hi, k - HT + 1)
                dve.tensor_tensor(h_lo[:, k, :], merged[:, k, :], h_hi[:, k, :], SUB).then_inc(m_lo_dve, 1)
            for f in range(KT - 1):
                if f < KT - 2:
                    dve.wait_ge(units_done, 2 * P_WO + f + 1)
                    dve.scalar_tensor_tensor(xT[:, f, :], bank[WO_BANK[f]][:, :], mod[:, 2 * KT + f:2 * KT + f + 1],
                                             xT[:, f, :], MUL, ADD).then_inc(b_free if f in (4, 5) else x2_done, 1)
                if f >= 1:
                    g_ = f - 1
                    if g_ in (2, 3):
                        dve.wait_ge(a_free, g_ - 1)
                    else:
                        dve.wait_ge(x2_sq, g_ + 1 if g_ < 2 else g_ - 1)
                    square_add(dve, g_, sum_done, y_buf, b_buf, ADD)

            def residual_half(i):
                c, f, src = WO_HALVES[i]
                if c == 0:
                    dve.wait_ge(wo_half, i + 1)
                else:
                    dve.wait_ge(units_done, 2 * P_WO + f + 1)
                dve.scalar_tensor_tensor(xT[:, f, half(c)], bank[src][:, half(c)], mod[:, 2 * KT + f:2 * KT + f + 1],
                                         xT[:, f, half(c)], MUL, ADD).then_inc(x2_half, 1)

            def sum_of(i):
                c, f, _ = WO_HALVES[i]
                dve.wait_ge(sq_half, i + 1)
                if f == KT - 2:
                    dve.wait_ge(sum_done, KT - 3)
                else:
                    dve.wait_ge(sum_half, i)
                dve.tensor_tensor(y_buf[:, 0, half(c)], y_buf[:, 0, half(c)], b_buf[:, f % 2, half(c)],
                                  ADD).then_inc(sum_half, 1)

            def factors(c):
                dve.wait_ge(ss_done, c + 1)
                steps.link(dve.tensor_reduce(st[:, 0, 0:2], bank[6 + c][:, 0:HS].rearrange("p (b n) -> p b n", n=P),
                                             AX.X, ADD))
                variance(2, st[:, 0, 0:2], 1.0 / D)

            def diagonal(c):
                from_root(None, 0, 2 + KV + c, 2, st[:, 5, 0:2])
                for b in range(2):
                    t = c * HS + b * P
                    dve.tensor_scalar(y_buf[:, 1, t:t + P], ident[:, :], st[:, 5, b:b + 1], None,
                                      MUL).then_inc(diag_done, 1)

            def h2_scaled(m):
                c, f = m // KT, m % KT
                dve.wait_ge(r_done, c + 1)
                if f >= 4:
                    dve.wait_ge(*h2_signal(m - 4))
                dve.scalar_tensor_tensor(tb(f)[:, half(c)], xT[:, f, half(c)], amp[:, 1, f:f + 1],
                                         bank[1 - c][:, 0:HS], MUL, MUL).then_inc(t2_done, 1)

            def h2_low(m):
                c, f = m // KT, m % KT
                dve.wait_ge(h2_h, m + 1)
                dve.scalar_tensor_tensor(h_lo[:, f, half(c)], tb(f)[:, half(c)],
                                         mod[:, 3 * KT + f:3 * KT + f + 1], h_hi[:, f, half(c)],
                                         ADD, SUB).then_inc(h2_ready, 1)

            residual_half(0)
            sum_of(0)
            residual_half(1)
            sum_of(1)
            factors(0)
            diagonal(0)
            residual_half(2)
            h2_scaled(0)
            h2_scaled(1)
            sum_of(2)
            residual_half(3)
            for m in range(2, 2 * KT):
                if not by_pool(m - 2):
                    h2_low(m - 2)
                h2_scaled(m)
                if m == 2:
                    sum_of(3)
                if m == 4:
                    factors(1)
                if m == 6:
                    diagonal(1)
            h2_low(2 * KT - 2)
            h2_low(2 * KT - 1)

            with dve.Fori(0, FF // PC) as j:
                steps.enter(j, STEPS_UP)
                for u in range(2):
                    def w(row):
                        return par[:, bass.ds(j * 2 + (row + u), 1)]
                    dve.wait_ge(a_free, j * 2 + (2 + u + 1))
                    steps.link(dve.tensor_scalar(a_buf[:, u, :], pad[u][:, 0:S], w(PA_FW), w(PA_FB), MUL, ADD))
                    steps.link(dve.scalar_tensor_tensor(a_buf[:, u, :], pad[u][:, 1:S + 1], w(PA_FW + FT),
                                                        a_buf[:, u, :], MUL, ADD))
                    dve.scalar_tensor_tensor(a_buf[:, u, :], pad[u][:, 2:S + 2], w(PA_FW + 2 * FT), a_buf[:, u, :],
                                             MUL, ADD).then_inc(conv_done, 1)
                for u in range(2):
                    dve.wait_ge(f_sq, j * 2 + (u + 1))
                    dve.scalar_tensor_tensor(b_buf[:, u, :], b_buf[:, u, :], 1.0 / GELU_C, a_buf[:, u, :],
                                             ADD, MUL).then_inc(z_done, 1)
                for u in range(2):
                    dve.wait_ge(f_th, j * 2 + (u + 1))
                    steps.link(dve.scalar_tensor_tensor(y_buf[:, u, :], b_buf[:, u, :], 1.0, a_buf[:, u, :], ADD, MUL))
                for u in range(2):
                    dve.wait_ge(units_done, j * 4 + (2 * P_UP + 2 + u + 1))
                    dve.scalar_tensor_tensor(y_buf[:, u, :], bank[4 + u][:, :], 0.5, y_buf[:, u, :],
                                             MUL, MUL).then_inc(b_free, 1)
                for u in range(2):
                    hi = g_hi[:, bass.ds(j * 2 + u, 1), :].rearrange("p a n -> p (a n)")
                    lo = g_lo[:, bass.ds(j * 2 + u, 1), :].rearrange("p a n -> p (a n)")
                    dve.wait_ge(b_free, j * 2 + (2 + u + 1))
                    steps.link(dve.tensor_scalar(hi, y_buf[:, u, :], 1.0, None, MUL))
                    dve.tensor_tensor(lo, y_buf[:, u, :], hi, SUB).then_inc(ffn_tiles, 1)
                steps.leave(FF // PC)

            with dve.Fori(0, 2) as i:
                for q in range(2):
                    for u in range(2):
                        f = 2 * q + u
                        dve.wait_ge(units_done, i * 12 + (2 * P_DOWN + 6 * q + 4 + u + 1))
                        dve.scalar_tensor_tensor((a_buf, y_buf)[q][:, u, :], bank[2 * q + u][:, :],
                                                 mod[:, bass.ds(i * 4 + (5 * KT + f), 1)],
                                                 xT[:, bass.ds(i * 4 + f, 1), :].rearrange("p a n -> p (a n)"),
                                                 MUL, ADD).then_inc(ffn_tiles, 1)


def square_add(dve, f, sum_done, y_buf, b_buf, ADD):
    if f == 0:
        return
    if f == 1:
        ins = dve.tensor_tensor(y_buf[:, 0, :], b_buf[:, 0, :], b_buf[:, 1, :], ADD)
    else:
        dve.wait_ge(sum_done, f - 1)
        ins = dve.tensor_tensor(y_buf[:, 0, :], y_buf[:, 0, :], b_buf[:, f % 2, :], ADD)
    ins.then_inc(sum_done, 1)


_INS = ["x", "c", "w_ada", "b_ada", "norm1_gain", "w_in", "conv_w", "q_gain", "k_gain", "sink", "w_o",
        "norm2_gain", "w_up", "ffn_conv_w", "ffn_conv_b", "w_down"]


def kernel(**inputs):
    import numpy as _np
    import concourse.bacc as _bacc
    from concourse import mybir as _mybir
    from concourse.bass_utils import run_bass_kernel_spmd as _run

    nc = _bacc.Bacc("TRN2", target_bir_lowering=False, num_devices=1)
    arrays, args = {}, []
    for name in _INS:
        a = _np.ascontiguousarray(inputs[name])
        arrays[f"in_{name}_dram"] = a
        args.append(nc.dram_tensor(f"in_{name}_dram", a.shape, _mybir.dt.from_np(a.dtype), kind="ExternalInput").ap())
    shape = inputs["x"].shape
    out = nc.dram_tensor("out_0_dram", shape, _mybir.dt.float32, kind="ExternalOutput").ap()
    encoder_block(nc, *args, out)
    r = _run(nc, [arrays], core_ids=[0])
    return r.results[0]["out_0_dram"]
```
